# Optimizing a Trainium2 kernel written in Bass

```python
import jax, jax.numpy as jnp
from jax import lax
import numpy as np

D_MODEL = 1024
BATCH = 1
SEQ = 1024
DEPTH = 1
DEC_BATCH = 8
DEC_SEQ = 4
PAST_LEN = 8192
PAGE_SIZE = 128

D_CONV = D_MODEL // 2
CONV_WIDTH = 31
GLA_HEADS = 4
GLA_DK = D_MODEL // 8
GLA_DV = D_MODEL // 4
GLA_RANK = 16
GLA_GATE_NORM = 16.0
GLA_CHUNK = 16
QK_W = GLA_HEADS * GLA_DK
V_W = GLA_HEADS * GLA_DV
N_GROUPS = 4
EXPERTS_PER_GROUP = 8
N_EXPERTS = N_GROUPS * EXPERTS_PER_GROUP
TOP_K = 2
D_EXPERT = D_MODEL // 2
ROUTE_BLOCK = 128
EPS = 1e-6
IN_SPLITS = (2 * D_CONV, QK_W, QK_W, V_W, V_W, GLA_RANK, D_MODEL, D_MODEL)
IN_WIDTH = sum(IN_SPLITS)

kernel_name = "hybrid_conv_gla_hiermoe_step"

def rms_norm(x, g):
    xf = x.astype(jnp.float32)
    y = xf * lax.rsqrt(jnp.mean(xf * xf, axis=-1, keepdims=True) + EPS)
    return (y * g.astype(jnp.float32)).astype(x.dtype)

def conformer_conv(u_in, buf, conv_dw, conv_db, ln_g, ln_b, w_pw):
    a, b = jnp.split(u_in, 2, axis=-1)
    u = a * jax.nn.sigmoid(b)
    full = jnp.concatenate([buf.astype(u.dtype), u], axis=1)
    y = lax.conv_general_dilated(full, conv_dw[:, None, :].astype(u.dtype), window_strides=(1,),
                                 padding='VALID', dimension_numbers=('NWC', 'WIO', 'NWC'),
                                 feature_group_count=D_CONV) + conv_db
    yf = y.astype(jnp.float32)
    mu = jnp.mean(yf, axis=-1, keepdims=True)
    var = jnp.mean(jnp.square(yf - mu), axis=-1, keepdims=True)
    yn = ((yf - mu) * lax.rsqrt(var + EPS) * ln_g + ln_b).astype(u.dtype)
    out = jax.nn.silu(yn) @ w_pw
    return out, full[:, -(CONV_WIDTH - 1):]

def gla_recurrence(q, k, v, log_a, s0, chunk):
    B, L = q.shape[:2]
    n = L // chunk

    def to_chunks(t):
        return t.astype(jnp.float32).reshape(B, n, chunk, GLA_HEADS, t.shape[-1]).transpose(1, 0, 3, 2, 4)

    qc, kc, vc, gc = to_chunks(q), to_chunks(k), to_chunks(v), to_chunks(log_a)
    causal = jnp.tril(jnp.ones((chunk, chunk), dtype=bool))[:, :, None]

    def step(s, inp):
        q_, k_, v_, g_ = inp
        b = jnp.cumsum(g_, axis=2)
        o_inter = jnp.einsum('bhtk,bhkv->bhtv', q_ * jnp.exp(b), s)
        diff = b[:, :, :, None, :] - b[:, :, None, :, :]
        decay = jnp.exp(jnp.where(causal, diff, -jnp.inf))
        att = jnp.einsum('bhtk,bhsk,bhtsk->bhts', q_, k_, decay)
        o = o_inter + jnp.einsum('bhts,bhsv->bhtv', att, v_)
        b_last = b[:, :, -1:, :]
        s_new = jnp.exp(b_last[:, :, 0, :])[..., None] * s + jnp.einsum(
            'bhsk,bhsv->bhkv', k_ * jnp.exp(b_last - b), v_)
        return s_new, o

    s_fin, o = lax.scan(step, s0.astype(jnp.float32), (qc, kc, vc, gc))
    o = o.transpose(1, 0, 3, 2, 4).reshape(B, L, GLA_HEADS, GLA_DV)
    return o, s_fin

def hier_moe(x, w_rg, b_rg, w_re, b_re, w_g, w_u, w_d):
    shp = x.shape
    xt = x.reshape(-1, D_MODEL)
    T = xt.shape[0]
    xf = xt.astype(jnp.float32)
    p_group = jax.nn.softmax(xf @ w_rg.astype(jnp.float32) + b_rg.astype(jnp.float32), axis=-1)
    g_idx = jnp.argmax(p_group, axis=-1)
    p_sel = jnp.take_along_axis(p_group, g_idx[:, None], axis=1)
    e_logits = (xf @ w_re.astype(jnp.float32) + b_re.astype(jnp.float32)).reshape(T, N_GROUPS, EXPERTS_PER_GROUP)
    e_logits = jnp.take_along_axis(e_logits, g_idx[:, None, None], axis=1)[:, 0]
    top_v, top_i = lax.top_k(e_logits, TOP_K)
    w_pair = p_sel * jax.nn.softmax(top_v, axis=-1)
    eid = (g_idx[:, None] * EXPERTS_PER_GROUP + top_i).reshape(-1).astype(jnp.int32)
    tok = jnp.arange(T * TOP_K, dtype=jnp.int32) // TOP_K
    wt = w_pair.reshape(-1)
    order = jnp.argsort(eid)
    eid_s, tok_s, wt_s = eid[order], tok[order], wt[order]
    counts = jnp.bincount(eid, length=N_EXPERTS)
    padded = (counts + ROUTE_BLOCK - 1) // ROUTE_BLOCK * ROUTE_BLOCK
    raw_start = jnp.cumsum(counts) - counts
    pad_end = jnp.cumsum(padded)
    pad_start = pad_end - padded
    dest = pad_start[eid_s] + (jnp.arange(T * TOP_K, dtype=jnp.int32) - raw_start[eid_s])
    n_blocks = -(-(T * TOP_K) // ROUTE_BLOCK) + N_EXPERTS
    n_rows = n_blocks * ROUTE_BLOCK
    row_tok = jnp.zeros((n_rows,), jnp.int32).at[dest].set(tok_s)
    row_wt = jnp.zeros((n_rows,), jnp.float32).at[dest].set(wt_s)
    block_e = jnp.minimum(jnp.searchsorted(pad_end, jnp.arange(n_blocks) * ROUTE_BLOCK, side='right'),
                          N_EXPERTS - 1)
    xb = xt[row_tok].reshape(n_blocks, ROUTE_BLOCK, D_MODEL)

    def expert_block(args):
        xblk, e = args
        hidden = jax.nn.silu(xblk @ w_g[e]) * (xblk @ w_u[e])
        return hidden @ w_d[e]

    yb = lax.map(expert_block, (xb, block_e))
    y = jax.ops.segment_sum(yb.reshape(n_rows, D_MODEL).astype(jnp.float32) * row_wt[:, None],
                            row_tok, num_segments=T)
    return y.astype(x.dtype).reshape(shp)

def decoder_layer(x, conv_buf, gla_s, norm_mix, w_in, b_gates, w_gla_gate_up, b_gla_gate_up,
                  conv_dw, conv_db, conv_ln_g, conv_ln_b, w_conv_out, gla_norm_g, w_gla_out, w_out,
                  norm_ffn, w_router_group, b_router_group, w_router_expert, b_router_expert,
                  w_expert_gate, w_expert_up, w_expert_down):
    B, L, _ = x.shape
    hn = rms_norm(x, norm_mix)
    proj = hn @ w_in
    split_points = np.cumsum(np.array(IN_SPLITS))[:-1].tolist()
    u_glu, q, k, v, r, a_low, gate_c, gate_g = jnp.split(proj, split_points, axis=-1)
    conv_out, new_buf = conformer_conv(u_glu, conv_buf, conv_dw, conv_db, conv_ln_g, conv_ln_b, w_conv_out)
    log_a = jax.nn.log_sigmoid((a_low @ w_gla_gate_up + b_gla_gate_up).astype(jnp.float32)) / GLA_GATE_NORM
    chunk = GLA_CHUNK if L % GLA_CHUNK == 0 else L
    o, new_s = gla_recurrence(q.reshape(B, L, GLA_HEADS, GLA_DK) * (GLA_DK ** -0.5),
                              k.reshape(B, L, GLA_HEADS, GLA_DK),
                              v.reshape(B, L, GLA_HEADS, GLA_DV),
                              log_a.reshape(B, L, GLA_HEADS, GLA_DK), gla_s, chunk)
    o = rms_norm(o.astype(x.dtype), gla_norm_g.reshape(GLA_HEADS, GLA_DV)).reshape(B, L, V_W)
    gla_out = (o * jax.nn.silu(r)) @ w_gla_out
    gc = jax.nn.sigmoid(gate_c + b_gates[:D_MODEL])
    gg = jax.nn.sigmoid(gate_g + b_gates[D_MODEL:])
    h = x + (gc * conv_out + gg * gla_out) @ w_out
    h = h + hier_moe(rms_norm(h, norm_ffn), w_router_group, b_router_group, w_router_expert,
                     b_router_expert, w_expert_gate, w_expert_up, w_expert_down)
    return h, new_buf.astype(x.dtype), new_s.astype(x.dtype)

def setup_inputs(seed: int = 0) -> dict:
    key = jax.random.key(seed)
    ks = jax.random.split(key, 32)
    f32 = jnp.float32
    nrm = lambda k, shape, s: jax.random.normal(k, shape, f32) * s
    L_ = DEPTH
    return {
        "x_prompt": nrm(ks[0], (BATCH, SEQ, D_MODEL), 1.0),
        "x_sample": nrm(ks[1], (DEC_BATCH, DEC_SEQ, D_MODEL), 1.0),
        "state_conv": nrm(ks[2], (L_, DEC_BATCH, CONV_WIDTH - 1, D_CONV), 0.5),
        "state_gla": nrm(ks[3], (L_, DEC_BATCH, GLA_HEADS, GLA_DK, GLA_DV), 0.3),
        "norm_mix": 1.0 + nrm(ks[4], (L_, D_MODEL), 0.02),
        "w_in": nrm(ks[5], (L_, D_MODEL, IN_WIDTH), D_MODEL ** -0.5),
        "b_gates": nrm(ks[6], (L_, 2 * D_MODEL), 0.02),
        "w_gla_gate_up": nrm(ks[7], (L_, GLA_RANK, QK_W), GLA_RANK ** -0.5),
        "b_gla_gate_up": nrm(ks[8], (L_, QK_W), 0.1),
        "conv_dw": nrm(ks[9], (L_, CONV_WIDTH, D_CONV), CONV_WIDTH ** -0.5),
        "conv_db": nrm(ks[10], (L_, D_CONV), 0.02),
        "conv_ln_g": 1.0 + nrm(ks[11], (L_, D_CONV), 0.02),
        "conv_ln_b": nrm(ks[12], (L_, D_CONV), 0.02),
        "w_conv_out": nrm(ks[13], (L_, D_CONV, D_MODEL), D_CONV ** -0.5),
        "gla_norm_g": 1.0 + nrm(ks[14], (L_, V_W), 0.02),
        "w_gla_out": nrm(ks[15], (L_, V_W, D_MODEL), V_W ** -0.5),
        "w_out": nrm(ks[16], (L_, D_MODEL, D_MODEL), D_MODEL ** -0.5),
        "norm_ffn": 1.0 + nrm(ks[17], (L_, D_MODEL), 0.02),
        "w_router_group": nrm(ks[18], (L_, D_MODEL, N_GROUPS), D_MODEL ** -0.5),
        "b_router_group": nrm(ks[19], (L_, N_GROUPS), 0.01),
        "w_router_expert": nrm(ks[20], (L_, D_MODEL, N_EXPERTS), D_MODEL ** -0.5),
        "b_router_expert": nrm(ks[21], (L_, N_EXPERTS), 0.01),
        "w_expert_gate": nrm(ks[22], (L_, N_EXPERTS, D_MODEL, D_EXPERT), D_MODEL ** -0.5),
        "w_expert_up": nrm(ks[23], (L_, N_EXPERTS, D_MODEL, D_EXPERT), D_MODEL ** -0.5),
        "w_expert_down": nrm(ks[24], (L_, N_EXPERTS, D_EXPERT, D_MODEL), D_EXPERT ** -0.5),
        "norm_final": 1.0 + nrm(ks[25], (D_MODEL,), 0.02),
    }

def reference(x_prompt, x_sample, state_conv, state_gla, norm_mix, w_in, b_gates, w_gla_gate_up,
              b_gla_gate_up, conv_dw, conv_db, conv_ln_g, conv_ln_b, w_conv_out, gla_norm_g, w_gla_out,
              w_out, norm_ffn, w_router_group, b_router_group, w_router_expert, b_router_expert,
              w_expert_gate, w_expert_up, w_expert_down, norm_final):
    hp, hs = x_prompt, x_sample
    bp = x_prompt.shape[0]
    conv_p, gla_p, conv_s, gla_s = [], [], [], []
    for l in range(DEPTH):
        params = (norm_mix[l], w_in[l], b_gates[l], w_gla_gate_up[l], b_gla_gate_up[l], conv_dw[l],
                  conv_db[l], conv_ln_g[l], conv_ln_b[l], w_conv_out[l], gla_norm_g[l], w_gla_out[l],
                  w_out[l], norm_ffn[l], w_router_group[l], b_router_group[l], w_router_expert[l],
                  b_router_expert[l], w_expert_gate[l], w_expert_up[l], w_expert_down[l])
        buf0 = jnp.zeros((bp, CONV_WIDTH - 1, D_CONV), x_prompt.dtype)
        s0 = jnp.zeros((bp, GLA_HEADS, GLA_DK, GLA_DV), jnp.float32)
        hp, cb, sb = decoder_layer(hp, buf0, s0, *params)
        conv_p.append(cb)
        gla_p.append(sb)
        hs, cb, sb = decoder_layer(hs, state_conv[l], state_gla[l], *params)
        conv_s.append(cb)
        gla_s.append(sb)
    y_prompt = rms_norm(hp, norm_final)
    y_sample = rms_norm(hs, norm_final)
    new_conv_prompt = jnp.stack(conv_p, axis=0)
    new_gla_prompt = jnp.stack(gla_p, axis=0)
    new_conv_sample = jnp.stack(conv_s, axis=0)
    new_gla_sample = jnp.stack(gla_s, axis=0)
    return (y_prompt, y_sample, new_conv_prompt, new_gla_prompt, new_conv_sample, new_gla_sample)


_drawn_inputs = setup_inputs


def setup_inputs(seed=0):
    import zlib

    import numpy as np

    out = dict(_drawn_inputs(seed))
    spreads = {}
    factors = {'b_gates': 4.414,
     'conv_ln_b': 12.061,
     'gla_norm_g': 14.589,
     'b_router_group': 13.693,
     'b_router_expert': 15.347,
     'norm_final': 22.025,
     'conv_db': 3.282,
     'conv_ln_g': 12.45,
     'norm_ffn': 4.253}
    for name, (base, spread) in spreads.items():
        noise = np.random.default_rng([zlib.crc32(name.encode()), seed]).standard_normal(out[name].shape)
        drawn = base * np.exp(spread * noise) if base else spread * noise
        out[name] = __import__('jax').numpy.asarray(drawn.astype(out[name].dtype))
    for name, factor in factors.items():
        out[name] = (out[name] * factor).astype(out[name].dtype)
    return out
```

```python
from contextlib import ExitStack

import concourse.bass as bass
from concourse import mybir

F32 = mybir.dt.float32
I32 = mybir.dt.int32
U32 = mybir.dt.uint32
I8 = mybir.dt.int8
ALU = mybir.AluOpType
ACT = mybir.ActivationFunctionType
AX_X = mybir.AxisListType.X

P = 128
BIG = 3.0e38
EPS = 1e-6
GATE_NORM = 16.0
NO_PAIR = 4096


def hybrid_layer(nc, a, o):
    SEQ, D = a["x_prompt"].shape[1:]
    NB, NS = a["x_sample"].shape[:2]
    CW = a["conv_dw"].shape[1]
    DC = a["conv_dw"].shape[2]
    _, _, H, DK, DV = a["state_gla"].shape
    RANK = a["w_gla_gate_up"].shape[1]
    NE, _, DE = a["w_expert_gate"].shape[1:]
    NG = a["w_router_group"].shape[2]
    EG = NE // NG
    QK, VW = H * DK, H * DV
    S_T = NB * NS
    T = SEQ + S_T
    KC = D // P
    CC = DC // P
    FC = DE // P
    NCH = SEQ // P
    NT = NCH + 1
    BLK = T // 3
    LV = 7
    CAP = NT * P
    MAXX = 2 * T // (P + 1)
    NBX = NCH
    PAD = CW - 1
    UP = PAD + SEQ
    US = PAD + NS
    UW = UP + NB * US
    assert D == 1024 and T % 3 == 0 and BLK <= 512 and DK == P and DV == 256 and DE == 512
    C_B, C_Q, C_K = DC, 2 * DC, 2 * DC + QK
    C_V = C_K + QK
    C_R = C_V + VW
    C_A = C_R + VW
    C_G = C_A + RANK

    w_in = a["w_in"][0]
    xs_flat = a["x_sample"].rearrange("b s d -> (b s) d")
    xp_flat = a["x_prompt"][0]

    qkb_scr = nc.dram_tensor("qkb_scr", [3, H, P, T], F32).ap()
    vr_scr = nc.dram_tensor("vr_scr", [2, T, VW], F32).ap()
    gate_scr = nc.dram_tensor("gate_scr", [2 * KC, P, T], F32).ap()
    h_scr = nc.dram_tensor("h_scr", [T, D], F32).ap()
    xn_scr = nc.dram_tensor("xn_scr", [T, D], F32).ap()
    y_scr = nc.dram_tensor("y_scr", [2 * T, D], F32).ap()
    slot_scr = nc.dram_tensor("slot_scr", [NE * CAP, 2], I32).ap()
    more_scr = nc.dram_tensor("more_scr", [16, 4], I32).ap()

    ctx = ExitStack()
    with ctx:
        def sb(name, shape, dt=F32):
            return ctx.enter_context(nc.sbuf_tensor(name, shape, dt))

        def sem(name):
            return ctx.enter_context(nc.semaphore(name))

        SLOT = KC * 512
        wring = sb("wring", [P, 6, SLOT])
        uo = sb("uo", [P, KC, T])
        ybuf = sb("ybuf", [P, CC, T])
        vrbuf = sb("vrbuf", [P, 2, 2, VW])
        gwork = sb("gwork", [P, SLOT])
        qe = sb("qe", [P, H, P])
        kdT = sb("kdT", [P, H, P])
        kdn = sb("kdn", [P, H * P])
        attn = sb("attn", [P, H, P])
        state = sb("state", [P, H, DV])
        ebuf = sb("ebuf", [P, H, P])
        onorm = sb("onorm", [P, VW])
        stage = sb("stage", [P, 2, T])
        ident = sb("ident", [P, P])
        ones = sb("ones", [P, P])
        masks = sb("masks", [P, LV * 64 + P], I8)
        par = sb("par", [P, 48])
        rowmask = sb("rowmask", [P, NB])
        small = sb("small", [P, 96])
        wts = sb("wts", [P, NT, 2])
        macc = sb("macc", [P, NE])
        pay = sb("pay", [P, NT, 2, 2], I32)

        def flat(t):
            n = len(t.shape)
            if n == 2:
                return t[:, :]
            if n == 3:
                return t[:, :, :].rearrange("p a b -> p (a b)")
            return t[:, :, :, :].rearrange("p a b c -> p (a b c)")

        wslot = [wring[:, s, :].rearrange("p (k n) -> p k n", n=512) for s in range(6)]
        wide = [wring[:, s, :].rearrange("p (k n) -> p k n", n=D) for s in range(6)]
        w_late = flat(gwork).rearrange("p (k n) -> p k n", n=512)
        high = wring[:, 3:6, :].rearrange("p s n -> p (s n)")
        nT = high[:, 0:KC * T].rearrange("p (k t) -> p k t", t=T)
        mixT = nT
        qkb = [high[:, KC * T + 1536 * b:KC * T + 1536 * (b + 1)].rearrange("p (w h t) -> p w h t", w=3, h=H)
               for b in range(2)]
        ggate = [high[:, KC * T + 1080 * b:KC * T + 1080 * b + T] for b in range(2)]
        gw = [wring[:, 2, 2048 * b:2048 * (b + 1)].rearrange("p (k n) -> p k n", n=256) for b in range(2)]
        xt = [vrbuf[:, 0, b, :] for b in range(2)]
        xn = [vrbuf[:, 1, b, :] for b in range(2)]
        u = flat(uo)[:, 0:CC * UW].rearrange("p (c w) -> p c w", w=UW)
        oT = uo
        lev = flat(gwork)[:, 0:LV * H * P].rearrange("p (l n) -> p l n", l=LV)
        absz = [flat(gwork)[:, T * b:T * (b + 1)] for b in range(2)]
        minz = flat(gwork)[:, 2 * T:3 * T]
        sq = [flat(gwork)[:, CC * BLK * b:CC * BLK * (b + 1)].rearrange("p (c t) -> p c t", c=CC) for b in range(2)]
        st = [stage[:, b, :] for b in range(2)]
        st3 = [flat(stage)[:, 512 * b:512 * (b + 1)] for b in range(4)]
        alow = flat(vrbuf)[0:RANK, 2 * D + 0:2 * D + T]
        wal = flat(attn)[:, 0:KC * RANK].rearrange("p (k n) -> p k n", n=RANK)
        wup = flat(qe)[0:RANK, 0:QK]
        prow = flat(kdn)[0:P, 0:P]
        dwrow = flat(kdn)[0:P, P:2 * P]
        scrow = [flat(state)[:, 0:512], flat(state)[:, 512:1024]]
        newc = flat(onorm)[:, 0:CC * NB * PAD].rearrange("p (c n) -> p c n", c=CC)
        mean_w = gwork[:, 3872:3872 + P]
        dwT = gwork[:, 3 * T:3 * T + CW * CC]
        rp = flat(state)
        wr = rp[:, 0:KC * (NG + NE)].rearrange("p (k n) -> p k n", k=KC)
        br, nffn = rp[:, 288:324], rp[:, 324:332]
        iota_e, iota_g, slot0, upper = rp[:, 332:364], rp[:, 364:396], rp[:, 396:428], rp[:, 428:556]
        eps_t = small[:, 0:1]
        ss = [small[:, 1:2], small[:, 2:3]]
        rstd = [small[:, 3:4], small[:, 4:5]]
        ss4 = small[:, 5:9]
        rstd4 = small[:, 9:13]
        jidx = small[:, 13:14]

        banks = [ctx.enter_context(nc.psum_tensor(f"bank{i}", [P, 512], F32)) for i in range(8)]
        bk = [t[:, :] for t in banks]

        const_step = sem("const_step")
        const_ready = sem("const_ready")
        waits_carried = sem("waits_carried")
        par_loaded = sem("par_loaded")
        par_ready = sem("par_ready")
        x_loaded = [sem(f"x_loaded{b}") for b in range(2)]
        x_squared = sem("x_squared")
        x_rms = sem("x_rms")
        xn_made = sem("xn_made")
        xT_ready = sem("xT_ready")
        nT_made = sem("nT_made")
        w_loaded = [sem(f"w_loaded{s}") for s in range(6)]
        w_free = [sem(f"w_free{s}") for s in range(3)]
        late_loaded = sem("late_loaded")
        small_w = sem("small_w")
        a_loaded = sem("a_loaded")
        attn_zero = sem("attn_zero")
        further_iota = sem("further_iota")
        proj_ready = sem("proj_ready")
        taken = [sem(f"taken{b}") for b in range(2)]
        absz_made = sem("absz_made")
        ln_made = sem("ln_made")
        b_made = sem("b_made")
        b_spilled = [sem(f"b_spilled{b}") for b in range(2)]
        qk_staged = sem("qk_staged")
        st_spilled = [sem(f"st_spilled{b}") for b in range(2)]
        vr_ready = sem("vr_ready")
        vr_staged = sem("vr_staged")
        vr_spilled = [sem(f"vr_spilled{b}") for b in range(3)]
        u_padded = sem("u_padded")
        sc_loaded = sem("sc_loaded")
        sc_T = sem("sc_T")
        sc_taken = sem("sc_taken")
        u_made = sem("u_made")
        newc_made = sem("newc_made")
        newc_T = sem("newc_T")
        newc_staged = sem("newc_staged")
        newc_out = [sem(f"newc_out{b}") for b in range(3)]
        conv_made = sem("conv_made")
        mean_ready = sem("mean_ready")
        centred = sem("centred")
        squared = sem("squared")
        var_ready = sem("var_ready")
        std_ready = sem("std_ready")
        normed = sem("normed")
        y_ready = sem("y_ready")
        gw_loaded = [sem(f"gw_loaded{b}") for b in range(2)]
        gw_free = sem("gw_free")
        chunk_loaded = [sem(f"chunk_loaded{b}") for b in range(2)]
        vrc_loaded = [sem(f"vrc_loaded{b}") for b in range(2)]
        diff_made = sem("diff_made")
        exp_made = sem("exp_made")
        prep_made = sem("prep_made")
        lev_ready = sem("lev_ready")
        lev_taken = sem("lev_taken")
        gate_ready = sem("gate_ready")
        gate_taken = sem("gate_taken")
        o_ready = sem("o_ready")
        ds_ready = sem("ds_ready")
        s_made = sem("s_made")
        o_rms = sem("o_rms")
        on_made = sem("on_made")
        oT_ready = sem("oT_ready")
        oT_taken = sem("oT_taken")
        s_out = sem("s_out")
        s0_loaded = [sem(f"s0_loaded{b}") for b in range(2)]
        samp_loaded = sem("samp_loaded")
        qem_made = sem("qem_made")
        kdm_made = sem("kdm_made")
        s0_read = sem("s0_read")
        sds_ready = sem("sds_ready")
        snew_made = sem("snew_made")
        snew_out = [sem(f"snew_out{b}") for b in range(2)]
        gates_loaded = [sem(f"gates_loaded{b}") for b in range(2)]
        gates_sig = sem("gates_sig")
        conv_ready = sem("conv_ready")
        conv_taken = sem("conv_taken")
        gla_ready = sem("gla_ready")
        mix_made = sem("mix_made")
        hx_loaded = [sem(f"hx_loaded{b}") for b in range(2)]
        h_ready = sem("h_ready")
        h_made = sem("h_made")
        h_squared = sem("h_squared")
        hn_made = sem("hn_made")
        h_spilled = [sem(f"h_spilled{b}") for b in range(2)]
        hT_ready = sem("hT_ready")
        hnT_made = sem("hnT_made")
        logit_ready = sem("logit_ready")
        gmax_made = sem("gmax_made")
        gsum_made = sem("gsum_made")
        dtop_made = sem("dtop_made")
        etop_made = sem("etop_made")
        pick_made = sem("pick_made")
        rank_ready = sem("rank_ready")
        slot_made = sem("slot_made")
        table_filled = sem("table_filled")
        scattered = sem("scattered")
        count_ready = sem("count_ready")
        more_made = sem("more_made")
        more_stored = sem("more_stored")
        lists_loaded = sem("lists_loaded")
        lists_f = sem("lists_f")
        lists_T = sem("lists_T")
        lists_ready = sem("lists_ready")
        xg_loaded = [sem(f"xg_loaded{b}") for b in range(2)]
        xgT_ready = sem("xgT_ready")
        xeT_made = sem("xeT_made")
        eg_done = sem("eg_done")
        eu_done = sem("eu_done")
        sg_made = sem("sg_made")
        hid_made = sem("hid_made")
        hidT_ready = sem("hidT_ready")
        hidT_made = sem("hidT_made")
        ed_done = sem("ed_done")
        ey_taken = sem("ey_taken")
        yo_free = sem("yo_free")
        y_scattered = [sem(f"y_scattered{b}") for b in range(2)]
        more_w = sem("more_w")
        more_idx = sem("more_idx")
        moe_done = sem("moe_done")
        f_loaded = [sem(f"f_loaded{b}") for b in range(2)]
        nf_loaded = sem("nf_loaded")
        f_sum = sem("f_sum")
        f_rms = sem("f_rms")
        f_made = sem("f_made")
        f_out = [sem(f"f_out{b}") for b in range(2)]

        def rows(t):
            return P if t < NCH else S_T

        def x_tile(t):
            return xp_flat[t * P:(t + 1) * P, :] if t < NCH else xs_flat

        NPROJ = 1 + H + 4 * CC
        VRJ = 4 * NT
        moe = flat(uo)
        xg = [moe[:, D * b:D * (b + 1)] for b in range(2)]
        xeT = [moe[:, D * (2 + b):D * (3 + b)].rearrange("p (k t) -> p k t", t=P) for b in range(2)]
        yo = [moe[:, D * (4 + b):D * (5 + b)] for b in range(2)]
        sgate = moe[:, 6 * D:6 * D + DE]
        hid = moe[:, 6 * D + DE:7 * D]
        hidT = moe[:, 7 * D:7 * D + DE].rearrange("p (k t) -> p k t", t=P)
        hx = [vrbuf[:, 0, b, :] for b in range(2)]
        hh = [vrbuf[:, 1, b, :] for b in range(2)]
        hn = [flat(ybuf)[:, D * b:D * (b + 1)] for b in range(2)]
        hnT = [flat(ybuf)[:, D * (2 + b):D * (3 + b)].rearrange("p (k t) -> p k t", t=P) for b in range(2)]
        rs = flat(kdn)
        gl, gm8, ngm, psel = rs[:, 0:8], rs[:, 8:16], rs[:, 16:17], rs[:, 17:18]
        gif, gsum, dtop, etop = rs[:, 18:19], rs[:, 19:20], rs[:, 20:21], rs[:, 21:22]
        eif, e8 = rs[:, 22:24], rs[:, 24:32]
        el, off, mk0, mk1, msum, rk, slotf = (rs[:, 32:64], rs[:, 64:96], rs[:, 96:128], rs[:, 128:160],
                                              rs[:, 160:192], rs[:, 192:224], rs[:, 224:226])
        junk = rs[:, 256:288]
        gexp = rs[:, 288:292]
        mpick = [rs[:, 320 + 96 * b:320 + 96 * (b + 1)].rearrange("p (m e) -> p m e", m=3) for b in range(2)]
        ri = flat(attn).bitcast(U32)
        gi8, ei8 = ri[:, 0:8], ri[:, 8:16]
        sloti = flat(attn).bitcast(I32)[:, 16:16 + 2 * NT].rearrange("p (t k) -> p t k", k=2)
        lst_i = flat(ebuf).bitcast(I32)[0:NE, 0:2 * P]
        lst_f = flat(ebuf)[0:NE, 2 * P:4 * P]
        lst_tok = flat(kdT).bitcast(I32)[:, 0:NE]
        lst_pair = flat(kdT).bitcast(I32)[:, NE:2 * NE]
        col_tok = [flat(kdT).bitcast(I32)[:, 64 + b:65 + b] for b in range(2)]
        col_pair = [flat(kdT).bitcast(I32)[:, 66 + b:67 + b] for b in range(2)]
        more_col = flat(kdT).bitcast(I32)[:, 68:70]
        mw = flat(qe)
        NF = NE * NBX
        m_flag, m_rank = mw[0:16, 0:NF], mw[0:16, NF:2 * NF]
        m_eq, m_val = flat(attn)[0:16, 0:NF], flat(attn)[0:16, NF:2 * NF]
        m_base = flat(onorm)[0:16, 0:NF]
        m_e = flat(onorm)[0:16, NF:2 * NF]
        m_th = flat(onorm)[0:16, 2 * NF:3 * NF]
        m_one = flat(onorm)[0:16, 3 * NF:4 * NF]
        m_out = small[0:16, 16:20]
        m_int = small[0:16, 20:24].bitcast(I32)
        cnt = small[:, 32:32 + NE]
        fh = [wring[:, 2 * b, 0:D] for b in range(2)]
        f0 = [wring[:, 2 * b, D:2 * D] for b in range(2)]
        f1 = [wring[:, 2 * b, 2 * D:3 * D] for b in range(2)]
        fo = [wring[:, 2 * b, 3 * D:4 * D] for b in range(2)]
        nfin = wring[:, 1, 0:D]

        MS = ((2, 0, 1), (3, 4, 5))

        def settle(eng):
            eng.sem_inc(waits_carried, 1)

        def load_w(sp, kind, e, s, done):
            name = {"g": "w_expert_gate", "u": "w_expert_up", "d": "w_expert_down"}[kind]
            if isinstance(e, int):
                w = a[name][0, e]
                src = w.rearrange("(p k) n -> p (k n)", p=P)
            else:
                src = a[name][0, bass.ds(e, 1)].rearrange("e (p k) n -> p (e k n)", p=P)
            sp.dma_start(wring[:, s, :], src).then_inc(done, 16)

        def lev_qem():
            return flat(gwork)[:, 0:NB * H * S_T].rearrange("p (b h t) -> p b h t", b=NB, h=H)

        def lev_kdm():
            return [flat(gwork)[:, 1024 + 512 * b:1536 + 512 * b] for b in range(2)]

        def new_state(dve, b):
            dve.wait_ge(sds_ready, b + 1)
            if b >= 2:
                dve.wait_ge(snew_out[b % 2], 16 * (b // 2))
            for h in range(H):
                last = dve.scalar_tensor_tensor(
                    st[b % 2][:, h * DV:(h + 1) * DV], vrbuf[:, 1, b % 2, h * DV:(h + 1) * DV],
                    ebuf[:, h, b * NS + NS - 1:b * NS + NS], bk[h // 2][:, DV * (h % 2):DV * (h % 2 + 1)],
                    ALU.mult, ALU.add)
            last.then_inc(snew_made, 1)

        def pick(dve, t, r, mp):
            lg = bk[6]
            dve.tensor_tensor(gl[0:r, 0:NG], lg[0:r, 0:NG], br[0:r, 0:NG], ALU.add)
            dve.tensor_tensor(el[0:r, :], lg[0:r, NG:NG + NE], br[0:r, NG:NG + NE], ALU.add)
            dve.drain()
            dve.max(gm8[0:r, :], gl[0:r, :])
            dve.drain()
            dve.max_index(gi8[0:r, :], gm8[0:r, :], gl[0:r, :])
            dve.tensor_scalar(ngm[0:r, :], gm8[0:r, 0:1], -1.0, None, ALU.mult).then_inc(gmax_made, 1)
            dve.drain()
            dve.tensor_copy(gif[0:r, :], gi8[0:r, 0:1])
            dve.drain()
            dve.tensor_scalar(off[0:r, :], iota_g[0:r, :], gif[0:r, :], -BIG, ALU.not_equal, ALU.mult)
            dve.drain()
            dve.tensor_tensor(el[0:r, :], el[0:r, :], off[0:r, :], ALU.add)
            dve.drain()
            dve.max(e8[0:r, :], el[0:r, :])
            dve.drain()
            dve.tensor_tensor(dtop[0:r, :], e8[0:r, 1:2], e8[0:r, 0:1], ALU.subtract).then_inc(dtop_made, 1)
            dve.max_index(ei8[0:r, :], e8[0:r, :], el[0:r, :])
            dve.drain()
            dve.tensor_copy(eif[0:r, :], ei8[0:r, 0:2])
            dve.drain()
            for k in range(2):
                dve.tensor_scalar(mp[0:r, k, :], iota_e[0:r, :], eif[0:r, k:k + 1], None, ALU.is_equal)
            dve.drain()
            dve.tensor_tensor(mp[0:r, 2, :], mp[0:r, 0, :], mp[0:r, 1, :], ALU.add).then_inc(pick_made, 1)
            dve.wait_ge(gsum_made, t + 1)
            dve.wait_ge(etop_made, t + 1)
            dve.reciprocal(psel[0:r, :], gsum[0:r, :])
            dve.tensor_scalar(sume[0:r, :], etop[0:r, :], 1.0, None, ALU.add)
            dve.drain()
            dve.reciprocal(sume[0:r, :], sume[0:r, :])
            dve.drain()
            dve.tensor_tensor(wts[0:r, t, 0:1], psel[0:r, :], sume[0:r, :], ALU.mult)
            dve.drain()
            dve.tensor_tensor(wts[0:r, t, 1:2], wts[0:r, t, 0:1], etop[0:r, :], ALU.mult)

        sume = rs[:, 292:293]
        junk2 = flat(attn)[:, 64:96]
        stdb = [flat(gwork)[:, 2 * CC * BLK + BLK * j:2 * CC * BLK + BLK * (j + 1)] for j in range(3)]

        def u_parts(c, n):
            b0 = 3 * (n % 2)
            t2 = SEQ - 2 * BLK
            return [(u[:, c, PAD:PAD + BLK], bk[b0][:, 0:BLK]),
                    (u[:, c, PAD + BLK:PAD + 2 * BLK], bk[b0 + 1][:, 0:BLK]),
                    (u[:, c, PAD + 2 * BLK:UP], bk[b0 + 2][:, 0:t2]),
                    (u[:, c, UP:UW].rearrange("p (b w) -> p b w", w=US)[:, :, PAD:US],
                     bk[b0 + 2][:, t2:BLK].rearrange("p (b s) -> p b s", s=NS))]

        block = ctx.enter_context(nc.Block())

        @block.sync
        def _(sp):
            def cols(c0, n=512):
                return w_in[:, c0:c0 + n].rearrange("(k p) n -> p k n", p=P)

            with sp.Fori(0, NCH // 2) as i:
                for b in range(2):
                    sp.wait_ge(xn_made, i * 2 + b + 1)
                    sp.dma_start(xt[b], xp_flat[bass.ds(i * 256 + b * P, P), :]).then_inc(x_loaded[b], 16)
            sp.wait_ge(xn_made, NCH + 1)
            sp.dma_start(xt[0][0:S_T, :], xs_flat).then_inc(x_loaded[0], 16)
            sp.dma_start(wslot[0], cols(C_B)).then_inc(w_loaded[0], 16)
            sp.dma_start(wslot[1], cols(0)).then_inc(w_loaded[1], 16)
            for n, c0 in enumerate((C_Q, C_K, C_V, C_V + 512, C_R, C_R + 512)):
                sp.wait_ge(w_free[n % 2], n // 2 + 1)
                sp.dma_start(wslot[n % 2], cols(c0)).then_inc(w_loaded[n % 2], 16)
            for b in range(2):
                sp.dma_start(gw[b], cols(C_G + 256 * b, 256)).then_inc(gw_loaded[b], 16)
            sp.wait_ge(w_free[0], 4)
            sp.dma_start(wide[0], a["w_conv_out"][0].rearrange("(k p) n -> p k n", p=P)).then_inc(w_loaded[0], 16)
            sp.wait_ge(w_free[1], 4)
            sp.dma_start(wslot[1], a["w_gla_out"][0][:, 0:512].rearrange("(k p) n -> p k n", p=P)) \
              .then_inc(w_loaded[1], 16)
            for b in range(2):
                sp.wait_ge(b_spilled[b], 16 * (H // 2))
                sp.wait_ge(st_spilled[b], 16 * H)
            for b in range(3):
                sp.wait_ge(vr_spilled[b], 16 * VRJ // 3)

            def load_chunk(b, t0, n):
                for w in range(3):
                    sp.dma_start(qkb[b][:, w, :, 0:n], qkb_scr[w, :, :, t0].rearrange("h p t -> p h t")) \
                      .then_inc(chunk_loaded[b], 16)
                for w in range(2):
                    sp.dma_start(vrbuf[0:n, b, w, :], vr_scr[w, t0, :]).then_inc(vrc_loaded[b], 16)

            sp.wait_ge(proj_ready, 1 + H)
            for b in range(2):
                load_chunk(b, slice(b * P, (b + 1) * P), P)
            with sp.Fori(1, NCH // 2) as i:
                for b in range(2):
                    sp.wait_ge(oT_ready, i * 2 + b - 1)
                    load_chunk(b, bass.ds(i * 256 + b * P, P), P)
                    sp.wait_ge(gw_free, i * 2 + b - 1)
                    sp.dma_start(gw[b], w_in[:, bass.ds(C_G + i * 512 + 256 * b, 256)]
                                 .rearrange("(k p) n -> p k n", p=P)).then_inc(gw_loaded[b], 16)
            sp.wait_ge(oT_ready, NCH)
            load_chunk(0, slice(SEQ, T), S_T)
            for b in range(NB):
                if b >= 2:
                    sp.wait_ge(snew_made, b - 1)
                sp.dma_start(vrbuf[:, 1, b % 2, :].rearrange("p (h v) -> p h v", h=H),
                             a["state_gla"][0, b].rearrange("h k v -> k h v")).then_inc(s0_loaded[b % 2], 16)
            sp.wait_ge(gw_free, NCH)
            sp.dma_start(wslot[2], a["w_gla_out"][0][:, 512:D].rearrange("(k p) n -> p k n", p=P)) \
              .then_inc(w_loaded[2], 16)
            for b in range(2):
                sp.wait_ge(st_spilled[b], 16 * (H + KC))
                sp.wait_ge(snew_out[b], 16 * NB // 2)
            sp.wait_ge(on_made, NCH + 1)
            for j in range(KC):
                if j >= 2:
                    sp.wait_ge(mix_made, j - 1)
                sp.dma_start(st[j % 2], gate_scr[j]).then_inc(gates_loaded[j % 2], 16)
                sp.dma_start(ggate[j % 2], gate_scr[KC + j]).then_inc(gates_loaded[j % 2], 16)
                if j == 0:
                    sp.wait_ge(snew_made, NB)
                    sp.dma_start(w_late, a["w_out"][0][:, 0:512].rearrange("(k p) n -> p k n", p=P)) \
                      .then_inc(late_loaded, 16)
                if j == 5:
                    sp.wait_ge(w_free[1], 5)
                    sp.dma_start(wslot[1], a["w_out"][0][:, 512:D].rearrange("(k p) n -> p k n", p=P)) \
                      .then_inc(w_loaded[1], 16)
            for t in range(NT):
                if t >= 2:
                    sp.wait_ge(h_made, t - 1)
                sp.dma_start(hx[t % 2][0:rows(t), :], x_tile(t)).then_inc(hx_loaded[t % 2], 16)
                if t == 0:
                    sp.wait_ge(w_free[2], 1)
                    load_w(sp, "g", 0, 2, w_loaded[2])
                    sp.wait_ge(w_free[0], 5)
                    load_w(sp, "u", 0, 0, w_loaded[0])
            sp.wait_ge(w_free[1], 6)
            load_w(sp, "d", 0, 1, w_loaded[1])
            sp.wait_ge(h_ready, NT)
            load_w(sp, "g", 1, 3, w_loaded[3])
            load_w(sp, "u", 1, 4, w_loaded[4])
            load_w(sp, "d", 1, 5, w_loaded[5])
            sp.wait_ge(scattered, 16 * 2 * NT)
            sp.dma_start(lst_i, slot_scr.rearrange("(e s) w -> e s w", e=NE)[:, 0:P, :]
                         .rearrange("e s w -> e (s w)")).then_inc(lists_loaded, 16)
            with sp.Fori(1, NE // 2) as i:
                for b in range(2):
                    sg, su, sd = MS[b]
                    n = i * 2 + b
                    sp.wait_ge(eg_done, n - 1)
                    load_w(sp, "g", n, sg, w_loaded[sg])
                    sp.wait_ge(eu_done, n - 1)
                    load_w(sp, "u", n, su, w_loaded[su])
                    sp.wait_ge(ed_done, n - 1)
                    load_w(sp, "d", n, sd, w_loaded[sd])
            sp.wait_ge(ed_done, NE)
            sp.wait_ge(more_stored, 16)
            n_more = sp.value_load(more_scr[0:1, 2:3], min_val=0, max_val=MAXX)
            with sp.Fori(0, MAXX) as j:
                with sp.If(n_more > j):
                    e = sp.value_load(more_scr[bass.ds(j, 1), 1:2], min_val=0, max_val=NE - 1)
                    base = sp.value_load(more_scr[bass.ds(j, 1), 0:1], min_val=0, max_val=NE * CAP - P)
                    sp.wait_ge(ed_done, j + NE)
                    load_w(sp, "g", e, 2, more_w)
                    load_w(sp, "u", e, 0, more_w)
                    load_w(sp, "d", e, 1, more_w)
                    sp.dma_start(more_col, slot_scr[bass.ds(base, P), :]).then_inc(more_idx, 16)
                with sp.Else():
                    sp.nop()
                sp.nop()
            sp.wait_ge(moe_done, 1)
            sp.dma_start(nfin, a["norm_final"].rearrange("(a n) -> a n", a=1).broadcast_to([P, D])) \
              .then_inc(nf_loaded, 16)
            for t in range(NT):
                b, r = t % 2, rows(t)
                if t >= 2:
                    sp.wait_ge(f_made, t - 1)
                sp.dma_start(fh[b][0:r, :], h_scr[t * P:t * P + r, :]).then_inc(f_loaded[b], 16)
                sp.dma_start(f0[b][0:r, :], y_scr[t * P:t * P + r, :]).then_inc(f_loaded[b], 16)
                sp.dma_start(f1[b][0:r, :], y_scr[T + t * P:T + t * P + r, :]).then_inc(f_loaded[b], 16)
            for b in range(2):
                sp.wait_ge(f_out[b], 16 * ((NT + 1 - b) // 2))
            sp.wait_ge(s_out, 16)
            for b in range(3):
                sp.wait_ge(newc_out[b], 16)

        @block.gpsimd
        def _(pool):
            pool.dma_start(prow[0:16, :], a["b_gates"][0].rearrange("(r c) -> r c", c=P)).then_inc(par_loaded, 16)
            for r0, nm in ((16, "b_gla_gate_up"), (20, "conv_db"), (24, "conv_ln_g"), (28, "conv_ln_b"),
                           (32, "gla_norm_g"), (40, "norm_mix")):
                v = a[nm][0].rearrange("(r c) -> r c", c=P)
                pool.dma_start(prow[r0:r0 + v.shape[0], :], v).then_inc(par_loaded, 16)
            pool.dma_start(dwrow[0:CW * CC, :], a["conv_dw"][0].rearrange("w (c p) -> (w c) p", p=P)) \
                .then_inc(par_loaded, 16)
            pool.memset(ident[:, :], 0.0).then_inc(const_step, 1)
            pool.memset(mean_w[:, :], 1.0 / DC).then_inc(const_step, 1)
            pool.memset(ones[:, :], 1.0).then_inc(const_step, 1)
            pool.memset(masks[:, :], 1).then_inc(const_step, 1)
            pool.memset(rowmask[:, :], 1.0).then_inc(const_step, 1)
            pool.memset(eps_t, EPS).then_inc(const_step, 1)
            pool.memset(attn[:, :, :], 0.0).then_inc(const_step, 1)
            pool.wait_ge(const_step, 7)
            pool.dma_start(wal, w_in[:, C_A:C_A + RANK].rearrange("(k p) n -> p k n", p=P)).then_inc(a_loaded, 16)
            pool.dma_start(wup, a["w_gla_gate_up"][0]).then_inc(a_loaded, 16)
            pool.affine_select(out=ident[:, :], in_=ident[:, :], compare_op=ALU.not_equal, fill=1.0, base=0,
                               pattern=[[-1, P]], channel_multiplier=1).then_inc(const_ready, 1)
            pool.drain()
            for l in range(LV):
                m = 64 >> l
                v = masks[:, l * 64:(l + 1) * 64].rearrange("p (n i) -> p n i", i=m)
                pool.affine_select(out=v, in_=v, compare_op=ALU.is_ge, fill=0.0, base=0,
                                   pattern=[[-2 * m, 64 // m], [0, m]], channel_multiplier=1)
                pool.drain()
                pool.affine_select(out=v, in_=v, compare_op=ALU.is_ge, fill=0.0, base=m - 1,
                                   pattern=[[2 * m, 64 // m], [0, m]], channel_multiplier=-1)
                pool.drain()
            dg = masks[:, LV * 64:LV * 64 + P]
            pool.affine_select(out=dg, in_=dg, compare_op=ALU.is_equal, fill=0.0, base=0,
                               pattern=[[-1, P]], channel_multiplier=1)
            pool.affine_select(out=rowmask[:, :], in_=rowmask[:, :], compare_op=ALU.is_ge, fill=0.0, base=0,
                               pattern=[[-NS, NB]], channel_multiplier=1)
            pool.drain()
            pool.affine_select(out=rowmask[:, :], in_=rowmask[:, :], compare_op=ALU.is_ge, fill=0.0, base=NS - 1,
                               pattern=[[NS, NB]], channel_multiplier=-1)
            pool.iota(pay[:, :, :, :], [[P, NT], [0, 2], [0, 2]], base=0, channel_multiplier=1)
            pool.iota(jidx, [[0, 1]], base=1, channel_multiplier=1, allow_small_or_imprecise_dtypes=True)
            pool.memset(macc[:, :], 0.0)
            pool.drain()
            pool.iota(pay[:, :, 1, 1:2], [[P, NT]], base=T, channel_multiplier=1)
            pool.drain().then_inc(const_ready, 1)
            pool.memset(u[:, :, 0:PAD], 0.0).then_inc(u_padded, 1)
            for hf in range(2):
                pool.dma_start(scrow[hf][0:4 * PAD, :], a["state_conv"][0, 4 * hf:4 * hf + 4]
                               .rearrange("b w c -> (b w) c")).then_inc(sc_loaded, 16)
            fill = flat(ybuf).bitcast(I32)[:, 0:NE * CAP * 2 // P].rearrange("p (s w) -> p s w", w=2)
            pool.memset(fill[:, :, 0:1], 0)
            pool.memset(fill[:, :, 1:2], NO_PAIR)
            pool.drain()
            pool.dma_start(slot_scr.rearrange("(p s) w -> p (s w)", p=P), fill.rearrange("p s w -> p (s w)")) \
                .then_inc(table_filled, 16)
            for h in range(H):
                pool.wait_ge(b_made, h + 1)
                pool.dma_start(qkb_scr[2, h], absz[h % 2]).then_inc(b_spilled[h % 2], 16)
            for n in range(2 * H):
                pool.wait_ge(qk_staged, n + 1)
                pool.dma_start(qkb_scr[n // H, n % H], st[n % 2]).then_inc(st_spilled[n % 2], 16)
            pool.wait_ge(proj_ready, 1)
            pool.memset(attn[:, :, :], 0.0).then_inc(attn_zero, 1)
            pool.wait_ge(u_made, CC)
            pool.wait_ge(sc_taken, 1)
            us = u[:, :, UP:UW].rearrange("p c (b w) -> p c b w", w=US)
            for c in range(CC):
                last = pool.tensor_copy(newc[:, c, :].rearrange("p (b w) -> p b w", w=PAD), us[:, c, :, NS:US])
            last.then_inc(newc_made, 1)
            for m in range(VRJ):
                col, t = divmod(m, NT)
                r = rows(t)
                pool.wait_ge(vr_staged, m + 1)
                pool.dma_start(vr_scr[col // 2, t * P:t * P + r, (col % 2) * 512:(col % 2) * 512 + 512],
                               st3[m % 3][0:r, :]).then_inc(vr_spilled[m % 3], 16)
            pool.wait_ge(newc_staged, 1)
            pool.dma_start(o["new_conv_prompt"][0, 0], st3[3][0:PAD, :]).then_inc(newc_out[0], 16)
            for hf in range(2):
                pool.wait_ge(newc_staged, 2 + hf)
                pool.dma_start(o["new_conv_sample"][0, 4 * hf:4 * hf + 4].rearrange("b w c -> (b w) c"),
                               st3[hf][0:4 * PAD, :]).then_inc(newc_out[1 + hf], 16)
            with pool.Fori(0, NCH) as c:
                for k in range(2):
                    pool.wait_ge(gate_taken, c * 6 + (3 * k + 5))
                    pool.dma_start(gate_scr[bass.ds(c * 2 + k, 1)].rearrange("a p t -> (a p) t"), st[k]) \
                        .then_inc(st_spilled[k], 16)
            pool.wait_ge(s_made, NCH + 1)
            pool.dma_start(o["new_gla_prompt"][0, 0].rearrange("h k v -> k h v"), state[:, :, :]).then_inc(s_out, 16)
            for b in range(NB):
                pool.wait_ge(snew_made, b + 1)
                pool.dma_start(o["new_gla_sample"][0, b].rearrange("h k v -> k h v"),
                               st[b % 2][:, 0:D].rearrange("p (h v) -> p h v", h=H)).then_inc(snew_out[b % 2], 16)
            pool.wait_ge(s_out, 16)
            pool.dma_start(wr[:, :, 0:NG], a["w_router_group"][0].rearrange("(p k) n -> p k n", p=P)) \
                .then_inc(small_w, 16)
            pool.dma_start(wr[:, :, NG:NG + NE], a["w_router_expert"][0].rearrange("(p k) n -> p k n", p=P)) \
                .then_inc(small_w, 16)
            pool.dma_start(br[:, 0:NG], a["b_router_group"].broadcast_to([P, NG])).then_inc(small_w, 16)
            pool.dma_start(br[:, NG:NG + NE], a["b_router_expert"].broadcast_to([P, NE])).then_inc(small_w, 16)
            pool.dma_start(nffn[:, :], a["norm_ffn"][0].rearrange("(p k) -> p k", p=P)).then_inc(small_w, 16)
            pool.affine_select(out=upper[:, :], in_=ones[:, :], compare_op=ALU.is_gt, fill=0.0, base=0,
                               pattern=[[1, P]], channel_multiplier=-1).then_inc(const_ready, 1)
            pool.iota(iota_e[:, :], [[1, NE]], base=0, channel_multiplier=0, allow_small_or_imprecise_dtypes=True)
            pool.iota(iota_g[:, :], [[1, NG], [0, EG]], base=0, channel_multiplier=0,
                      allow_small_or_imprecise_dtypes=True)
            pool.iota(slot0[:, :], [[CAP, NE]], base=0, channel_multiplier=0, allow_small_or_imprecise_dtypes=True)
            pool.drain().then_inc(const_ready, 1)
            pool.wait_ge(table_filled, 16)
            for t in range(NT + 2):
                if t < NT:
                    b, r = t % 2, rows(t)
                    pool.wait_ge(h_made, t + 1)
                    pool.dma_start(h_scr[t * P:t * P + r, :], hh[b][0:r, :]).then_inc(h_spilled[b], 16)
                    pool.wait_ge(hn_made, t + 1)
                    pool.dma_start(xn_scr[t * P:t * P + r, :], hn[b][0:r, :]).then_inc(h_spilled[b], 16)
                if t >= 2:
                    r = rows(t - 2)
                    pool.wait_ge(slot_made, t - 1)
                    for k in range(2):
                        pool.indirect_dma_start(
                            out=slot_scr, out_offset=bass.IndirectOffsetOnAxis(ap=sloti[0:r, t - 2, k:k + 1], axis=0),
                            in_=pay[0:r, t - 2, k, :], in_offset=None).then_inc(scattered, 16)
            it = {"channel_multiplier": 0, "allow_small_or_imprecise_dtypes": True}
            pool.iota(m_base, [[CAP, NE], [P, NBX]], base=P, **it)
            pool.iota(m_e, [[1, NE], [0, NBX]], base=0, **it)
            pool.iota(m_th, [[0, NE], [P, NBX]], base=P, **it)
            pool.memset(m_one, 1.0)
            pool.drain().then_inc(further_iota, 1)
            pool.wait_ge(more_made, 1)
            pool.dma_start(more_scr, m_int).then_inc(more_stored, 16)
            for b in range(2):
                pool.wait_ge(h_spilled[b], 32 * ((NT + 1 - b) // 2))
            pool.wait_ge(lists_ready, 1)
            pool.sem_inc(yo_free, 2)

            def gather(n, b):
                settle(pool)
                pool.tensor_copy(col_tok[b], lst_tok[:, n if isinstance(n, slice) else bass.ds(n, 1)])
                pool.drain()
                pool.indirect_dma_start(out=xg[b], out_offset=None, in_=xn_scr,
                                        in_offset=bass.IndirectOffsetOnAxis(ap=col_tok[b], axis=0)) \
                    .then_inc(xg_loaded[b], 16)

            def scatter(n, b, done):
                pool.tensor_copy(col_pair[b], lst_pair[:, n if isinstance(n, slice) else bass.ds(n, 1)])
                pool.drain()
                pool.wait_ge(ey_taken, n_plus(n, 2))
                settle(pool)
                pool.indirect_dma_start(out=y_scr, in_=yo[b], in_offset=None,
                                        out_offset=bass.IndirectOffsetOnAxis(ap=col_pair[b], axis=0),
                                        bounds_check=2 * T - 1, oob_is_err=False).then_inc(y_scattered[b], 16)
                pool.wait_ge(y_scattered[b], done)
                settle(pool)
                pool.sem_inc(yo_free, 1)

            def n_plus(n, k):
                return (n.start if isinstance(n, slice) else n) + k

            for b in range(2):
                gather(slice(b, b + 1), b)
            with pool.Fori(0, NE // 2 - 1) as i:
                for b in range(2):
                    pool.wait_ge(xgT_ready, i * 2 + b + 1)
                    gather(i * 2 + (b + 2), b)
                    scatter(i * 2 + b, b, i * 16 + 16)
            for n in range(NE - 2, NE):
                scatter(slice(n, n + 1), n % 2, 8 * NE)
            pool.wait_ge(more_stored, 16)
            n_more = pool.value_load(more_scr[0:1, 2:3], min_val=0, max_val=MAXX)
            with pool.Fori(0, MAXX) as j:
                with pool.If(n_more > j):
                    pool.wait_ge(more_idx, j * 16 + 16)
                    settle(pool)
                    pool.tensor_copy(col_tok[0], more_col[:, 0:1])
                    pool.tensor_copy(col_pair[0], more_col[:, 1:2])
                    pool.drain()
                    pool.indirect_dma_start(out=xg[0], out_offset=None, in_=xn_scr,
                                            in_offset=bass.IndirectOffsetOnAxis(ap=col_tok[0], axis=0)) \
                        .then_inc(xg_loaded[0], 16)
                    pool.wait_ge(ey_taken, j + (NE + 2))
                    settle(pool)
                    pool.indirect_dma_start(out=y_scr, in_=yo[0], in_offset=None,
                                            out_offset=bass.IndirectOffsetOnAxis(ap=col_pair[0], axis=0),
                                            bounds_check=2 * T - 1, oob_is_err=False) \
                        .then_inc(y_scattered[0], 16)
                    pool.wait_ge(y_scattered[0], j * 16 + (8 * NE + 16))
                    settle(pool)
                    pool.sem_inc(yo_free, 1)
                with pool.Else():
                    pool.nop()
                pool.nop()
            pool.sem_inc(moe_done, 1)
            for t in range(NT):
                b, r = t % 2, rows(t)
                pool.wait_ge(f_made, t + 1)
                dst = o["y_prompt"][0, t * P:t * P + r, :] if t < NCH else o["y_sample"].rearrange("b s d -> (b s) d")
                pool.dma_start(dst, fo[b][0:r, :]).then_inc(f_out[b], 16)

        @block.tensor
        def _(pe):
            def mm(out, lhsT, rhs, start, stop, **kw):
                return pe.matmul(out, lhsT=lhsT, rhs=rhs, start=start, stop=stop, **kw)

            pe.wait_ge(const_ready, 1)
            pe.wait_ge(par_loaded, 16 * 8)
            pe.transpose(bk[6][:, 0:48], prow[0:48, :], ident[0:48, 0:48])
            pe.transpose(bk[6][:, 64:64 + CW * CC], dwrow[0:CW * CC, :], ident[0:CW * CC, 0:CW * CC]) \
              .then_inc(par_ready, 1)

            def x_transposes(b, r, wait):
                pe.wait_ge(xn_made, wait)
                for k in range(KC):
                    last = pe.transpose(bk[2 * b + k // 4][:, P * (k % 4):P * (k % 4) + r],
                                        xn[b][0:r, k * P:(k + 1) * P], ident[0:r, 0:r])
                last.then_inc(xT_ready, 1)

            with pe.Fori(0, NCH // 2) as i:
                for b in range(2):
                    pe.wait_ge(nT_made, i * 2 + b + 1)
                    x_transposes(b, P, i * 2 + b + 3)
            pe.wait_ge(nT_made, NCH + 1)
            x_transposes(0, S_T, NCH + 3)

            def project(n, lhs, rhs, m, ks):
                if n >= 2:
                    pe.wait_ge(taken[n % 2], n // 2)
                for j in range(3):
                    for k in range(ks):
                        last = mm(bk[3 * (n % 2) + j][0:m, 0:BLK], lhs(k), rhs(k)[:, j * BLK:(j + 1) * BLK],
                                  k == 0, k == ks - 1)
                return last.then_inc(proj_ready, 1)

            pe.wait_ge(nT_made, NT + 2)
            pe.wait_ge(a_loaded, 32)
            project(0, lambda k: wal[:, k, :], lambda k: nT[:, k, :], RANK, KC)
            pe.wait_ge(taken[0], 1)
            for h in range(H):
                project(1 + h, lambda k: wup[:, h * DK:(h + 1) * DK], lambda k: alow, P, 1)
            n = 1 + H
            for s in range(4):
                pe.wait_ge(w_loaded[s % 2], 16 * (s // 2 + 1))
                for j in range(CC):
                    last = project(n, lambda k: wslot[s % 2][:, k, j * P:(j + 1) * P], lambda k: nT[:, k, :], P, KC)
                    n += 1
                pe.drain().then_inc(w_free[s % 2], 1)
                if s == 1:
                    pe.wait_ge(sc_loaded, 32)
                    for hf in range(2):
                        for c in range(CC):
                            last = pe.transpose(bk[6 + hf][:, c * 4 * PAD:(c + 1) * 4 * PAD],
                                                scrow[hf][0:4 * PAD, c * P:(c + 1) * P],
                                                ident[0:4 * PAD, 0:4 * PAD])
                    last.then_inc(sc_T, 1)
            assert n == NPROJ
            for b in range(2):
                pe.wait_ge(taken[b], (NPROJ + 1 - b) // 2)
            for m in range(VRJ):
                col, t = divmod(m, NT)
                r = rows(t)
                if t == 0:
                    pe.wait_ge(w_loaded[col % 2], 16 * (col // 2 + 3))
                if m >= 6:
                    pe.wait_ge(vr_staged, m - 5)
                for k in range(KC):
                    last = mm(bk[m % 6][0:r, :], nT[:, k, t * P:t * P + r], wslot[col % 2][:, k, :],
                              k == 0, k == KC - 1)
                last.then_inc(vr_ready, 1)
                if t == NT - 1:
                    pe.drain().then_inc(w_free[col % 2], 1)
            pe.wait_ge(newc_made, 1)
            pe.wait_ge(sc_taken, 1)
            for c in range(CC):
                last = pe.transpose(bk[6][0:PAD, c * P:(c + 1) * P], u[:, c, UP - PAD:UP], ident[:, :])
            last.then_inc(newc_T, 1)
            for hf in range(2):
                if hf:
                    pe.wait_ge(newc_staged, 1)
                for c in range(CC):
                    last = pe.transpose(bk[7 - hf][0:4 * PAD, c * P:(c + 1) * P],
                                        newc[:, c, 4 * PAD * hf:4 * PAD * (hf + 1)], ident[:, :])
                last.then_inc(newc_T, 1)
            pe.wait_ge(conv_made, 1)
            pe.wait_ge(vr_staged, VRJ)
            for j in range(3):
                for c in range(CC):
                    last = mm(bk[2 * j][:, 0:BLK], mean_w[:, :], ybuf[:, c, j * BLK:(j + 1) * BLK], c == 0, c == CC - 1)
                last.then_inc(mean_ready, 1)
            for j in range(3):
                pe.wait_ge(squared, j + 1)
                for c in range(CC):
                    last = mm(bk[2 * j + 1][:, 0:BLK], mean_w[:, :], sq[j % 2][:, c, :], c == 0, c == CC - 1)
                last.then_inc(var_ready, 1)
            pe.wait_ge(normed, 3)

            def gate_block(c, b, k, j):
                g = k * 3 + j
                pe.wait_ge(gate_taken, c * 6 + (g + 1))
                for q in range(KC):
                    last = mm(bk[g % 2][:, 0:BLK], gw[b][:, q, k * P:(k + 1) * P],
                              nT[:, q, j * BLK:(j + 1) * BLK], q == 0, q == KC - 1)
                last.then_inc(gate_ready, 1)

            def chunk(c, b, i):
                pe.wait_ge(gw_loaded[b], i * 16 + 16)
                for j in range(3):
                    gate_block(c, b, 0, j)
                pe.wait_ge(prep_made, c + 1)
                lv = lev.rearrange("p l (h t) -> p l h t", h=H)
                for l in range(LV + 2):
                    x = (LV + 2) * b + l
                    pe.wait_ge(lev_taken, c * (LV + 2) + (l + 1))
                    dst = bk[2 + x % 2]
                    for h in range(H):
                        if l < LV:
                            m = 64 >> l
                            right = lv[:, l, h, :].rearrange("p (n z i) -> p n z i", z=2, i=m)[:, :, 1, :]
                            last = mm(dst[:, 64 * h:64 * h + 64].rearrange("p (n i) -> p n i", i=m),
                                      lv[:, l, h, :], right, True, True)
                        elif l == LV:
                            last = mm(dst[:, P * h:P * h + P], qkb[b][:, 1, h, :], qkb[b][:, 0, h, :], True, True)
                        else:
                            last = pe.transpose(dst[:, P * h:P * h + P], kdT[:, h, :], ident[:, :])
                    last.then_inc(lev_ready, 1)
                pe.wait_ge(lev_taken, c * (LV + 2) + (LV + 4))
                pe.wait_ge(s_made, c + 1)
                pe.wait_ge(vrc_loaded[b], i * 32 + 32)
                for h in range(H):
                    dst = bk[4 + h // 2][:, DV * (h % 2):DV * (h % 2 + 1)]
                    mm(dst, attn[:, h, :], vrbuf[:, b, 0, h * DV:(h + 1) * DV], True, False)
                    last = mm(dst, qe[:, h, :], state[:, h, :], False, True)
                last.then_inc(o_ready, 1)
                for h in range(H):
                    last = mm(bk[6 + h // 2][:, DV * (h % 2):DV * (h % 2 + 1)], kdn[:, h * P:(h + 1) * P],
                              vrbuf[:, b, 0, h * DV:(h + 1) * DV], True, True)
                last.then_inc(ds_ready, 1)
                for j in range(3):
                    gate_block(c, b, 1, j)
                pe.drain().then_inc(gw_free, 1)
                o_transposes(P, c + 1)
                pe.wait_ge(oT_taken, c + 1)

            def o_transposes(r, wait):
                pe.wait_ge(on_made, wait)
                for k in range(KC):
                    last = pe.transpose(bk[4 + k // 4][:, P * (k % 4):P * (k % 4) + r],
                                        onorm[0:r, k * P:(k + 1) * P], ident[0:r, 0:r])
                last.then_inc(oT_ready, 1)

            with pe.Fori(0, NCH // 2) as i:
                for b in range(2):
                    chunk(i * 2 + b, b, i)
            NL = NCH * (LV + 2)
            R = S_T
            pe.wait_ge(prep_made, NCH + 1)
            for x, l in enumerate((LV - 2, LV - 1, LV)):
                m = max(64 >> l, 1)
                if x >= 1:
                    pe.wait_ge(lev_taken, NL + 2 + x)
                for h in range(H):
                    if l < LV:
                        w = lev.rearrange("p l (h t) -> p l h t", h=H)[:, l, h, 0:R]
                        right = w.rearrange("p (n z i) -> p n z i", z=2, i=m)[:, :, 1, :]
                        last = mm(bk[2][0:R, 16 * h:16 * h + 16].rearrange("p (n i) -> p n i", i=m), w, right,
                                  True, True)
                    else:
                        last = mm(bk[2][0:R, R * h:R * h + R], qkb[0][:, 1, h, 0:R], qkb[0][:, 0, h, 0:R],
                                  True, True)
                last.then_inc(lev_ready, 1)
            pe.wait_ge(lev_taken, NL + 2 + 3)
            for h in range(H):
                last = pe.transpose(bk[2][0:R, P * h:P * h + P], kdT[:, h, 0:R], ident[:, :])
            last.then_inc(lev_ready, 1)
            pe.wait_ge(lev_taken, NL + 2 + 4)
            pe.wait_ge(gate_taken, 2 + 6 * NCH)
            pe.wait_ge(vrc_loaded[0], 32 * (NCH // 2 + 1))
            pe.wait_ge(s_made, 1 + NCH)
            for h in range(H):
                mm(bk[4 + h][0:R, 0:DV], attn[0:R, h, 0:R], vrbuf[0:R, 0, 0, h * DV:(h + 1) * DV], True, False,
                   skip_group_check=True)
            pe.wait_ge(qem_made, 1)
            qem = lev_qem()
            kdm = lev_kdm()
            for b in range(NB):
                pe.wait_ge(s0_loaded[b % 2], 16 * (b // 2 + 1))
                s0 = vrbuf[:, 1, b % 2, :].rearrange("p (h v) -> p h v", h=H)
                for h in range(H):
                    last = mm(bk[4 + h][0:R, 0:DV], qem[:, b, h, :], s0[:, h, :], False, b == NB - 1,
                              skip_group_check=True)
                if b == NB - 1:
                    last.then_inc(o_ready, 1)
                pe.wait_ge(kdm_made, b + 1)
                if b >= 1:
                    pe.wait_ge(snew_made, b)
                for h in range(H):
                    last = mm(bk[h // 2][:, DV * (h % 2):DV * (h % 2 + 1)], kdm[b % 2][0:R, h * P:(h + 1) * P],
                              vrbuf[0:R, 0, 0, h * DV:(h + 1) * DV], True, True)
                last.then_inc(sds_ready, 1)
            pe.wait_ge(on_made, NCH + 1)
            o_transposes(R, NCH + 1)

            pe.wait_ge(oT_taken, NCH + 1)
            pe.wait_ge(snew_made, NB)
            pe.wait_ge(y_ready, 3)
            pe.wait_ge(w_loaded[0], 16 * 5)
            for j in range(KC):
                if j:
                    pe.wait_ge(conv_taken, j)
                for q in range(3):
                    for k in range(CC):
                        last = mm(bk[q][:, 0:BLK], wide[0][:, k, j * P:(j + 1) * P],
                                  ybuf[:, k, q * BLK:(q + 1) * BLK], k == 0, k == CC - 1)
                last.then_inc(conv_ready, 1)
                if j:
                    pe.wait_ge(mix_made, j)
                if j == 0:
                    pe.wait_ge(w_loaded[1], 16 * 5)
                if j == 4:
                    pe.drain().then_inc(w_free[1], 1)
                    pe.wait_ge(w_loaded[2], 16)
                for q in range(3):
                    for k in range(KC):
                        last = mm(bk[3 + q][:, 0:BLK], wslot[1 + j // 4][:, k, (j % 4) * P:(j % 4 + 1) * P],
                                  oT[:, k, q * BLK:(q + 1) * BLK], k == 0, k == KC - 1)
                last.then_inc(gla_ready, 1)
            pe.drain().then_inc(w_free[2], 1)
            pe.drain().then_inc(w_free[0], 1)

            pe.wait_ge(mix_made, KC)
            pe.wait_ge(late_loaded, 16)
            pe.wait_ge(w_loaded[1], 16 * 6)
            pe.wait_ge(small_w, 16 * 5)
            pe.wait_ge(const_ready, 4)
            for t in range(NT + 2):
                if t < NT:
                    b, r = t % 2, rows(t)
                    if t >= 2:
                        pe.wait_ge(h_made, t - 1)
                    for hf, w in enumerate((w_late, wslot[1])):
                        for k in range(KC):
                            last = mm(bk[2 * b + hf][0:r, :], mixT[:, k, t * P:t * P + r], w[:, k, :],
                                      k == 0, k == KC - 1)
                    last.then_inc(h_ready, 1)
                    if t == NT - 1:
                        pe.drain().then_inc(w_free[1], 1)
                if 1 <= t <= NT:
                    b, r = (t - 1) % 2, rows(t - 1)
                    pe.wait_ge(hn_made, t)
                    if t >= 2:
                        pe.wait_ge(hnT_made, t - 1)
                    for k in range(KC):
                        last = pe.transpose(bk[4 + k // 4][:, P * (k % 4):P * (k % 4) + r],
                                            hn[b][0:r, k:D:KC], ident[0:r, 0:r])
                    last.then_inc(hT_ready, 1)
                    pe.wait_ge(hnT_made, t)
                    if t >= 2:
                        pe.wait_ge(pick_made, t - 1)
                    for k in range(KC):
                        last = mm(bk[6][0:r, 0:NG + NE], hnT[b][:, k, 0:r], wr[:, k, :], k == 0, k == KC - 1)
                    last.then_inc(logit_ready, 1)
                if t >= 2:
                    b, r = t % 2, rows(t - 2)
                    pe.wait_ge(pick_made, t - 1)
                    if t >= 3:
                        pe.wait_ge(slot_made, t - 2)
                    mm(bk[7][0:r, 0:NE], upper[0:r, 0:r], mpick[b][0:r, 2, :], True, False)
                    last = mm(bk[7][0:r, 0:NE], ones[:, 0:r], macc[:, :], False, True)
                    last.then_inc(rank_ready, 1)
            pe.wait_ge(slot_made, NT)
            mm(bk[7][:, 0:NE], ones[:, 0:P], macc[:, :], True, True).then_inc(count_ready, 1)
            pe.wait_ge(lists_f, 1)
            lf = lst_f.rearrange("e (s w) -> e s w", w=2)
            for w in range(2):
                last = pe.transpose(bk[6][:, P * w:P * w + NE], lf[:, :, w], ident[0:NE, 0:NE])
            last.then_inc(lists_T, 1)

            def x_expert(n, b, landed):
                pe.wait_ge(xg_loaded[b], landed)
                for k in range(KC):
                    last = pe.transpose(bk[k // 4][:, P * (k % 4):P * (k % 4 + 1)], xg[b][:, k:D:KC], ident[:, :])
                last.then_inc(xgT_ready, 1)

            def gate_up(n, b, wait_g, wait_u):
                sg, su, _ = MS[b]
                pe.wait_ge(xeT_made, n + 1)
                wait_g()
                for k in range(KC):
                    last = mm(bk[2], xeT[b][:, k, :], wslot[sg][:, k, :], k == 0, k == KC - 1)
                last.then_inc(eg_done, 1)
                wait_u()
                for k in range(KC):
                    last = mm(bk[3], xeT[b][:, k, :], wslot[su][:, k, :], k == 0, k == KC - 1)
                last.then_inc(eu_done, 1)

            def down(n, b, wait_d):
                pe.wait_ge(hid_made, n + 1)
                for k in range(FC):
                    last = pe.transpose(bk[4][:, P * k:P * (k + 1)], hid[:, k:DE:FC], ident[:, :])
                last.then_inc(hidT_ready, 1)
                wait_d()
                pe.wait_ge(hidT_made, n + 1)
                pe.wait_ge(ey_taken, n + 1)
                for hf in range(2):
                    for k in range(FC):
                        last = mm(bk[5 + hf], hidT[:, k, :], wide[MS[b][2]][:, k, hf * 512:(hf + 1) * 512],
                                  k == 0, k == FC - 1)
                last.then_inc(ed_done, 1)

            base = (16, 80, 96)
            def expert(n, b, i, nxt):
                waits = [(lambda s=s, q=q: pe.wait_ge(w_loaded[s], i * 16 + (16 + (base[q] if b == 0 else 0))))
                         for q, s in enumerate(MS[b])]
                gate_up(n, b, waits[0], waits[1])
                if nxt is not None:
                    x_expert(n + 1, 1 - b, nxt)
                down(n, b, waits[2])

            pe.wait_ge(lists_ready, 1)
            x_expert(0, 0, 16)
            with pe.Fori(0, NE // 2 - 1) as i:
                expert(i * 2, 0, i, i * 16 + 16)
                expert(i * 2 + 1, 1, i, i * 16 + 32)
            expert(NE - 2, 0, NE // 2 - 1, 8 * NE)
            expert(NE - 1, 1, NE // 2 - 1, None)
            pe.wait_ge(more_stored, 16)
            n_more = pe.value_load(more_scr[0:1, 2:3], min_val=0, max_val=MAXX)
            with pe.Fori(0, MAXX) as j:
                with pe.If(n_more > j):
                    x_expert(None, 0, j * 16 + (8 * NE + 16))
                    pe.wait_ge(more_w, j * 48 + 48)
                    gate_up(j + NE, 0, lambda: None, lambda: None)
                    down(j + NE, 0, lambda: None)
                with pe.Else():
                    pe.nop()
                pe.nop()

        @block.scalar
        def _(act):
            def f(out, in_, func, **kw):
                return act.activation(out, in_, func, **kw)

            act.wait_ge(const_ready, 2)
            act.sem_inc(gate_taken, 2)
            act.sem_inc(ey_taken, 1)

            def rms_tile(b, r, i2, loaded):
                act.wait_ge(x_loaded[b], loaded)
                act.wait_ge(nT_made, i2 + 1)
                f(xn[b][0:r, :], xt[b][0:r, :], ACT.Square, accum_out=ss[b][0:r, :])
                act.drain()
                f(rstd[b][0:r, :], ss[b][0:r, :], ACT.Sqrt, scale=1.0 / D, bias=eps_t[0:r, :]).then_inc(x_rms, 1)

            with act.Fori(0, NCH // 2) as i:
                for b in range(2):
                    rms_tile(b, P, i * 2 + b, i * 16 + 16)
            rms_tile(0, S_T, NCH, 16 * (NCH // 2 + 1))
            act.wait_ge(proj_ready, 1)
            for j in range(3):
                last = f(alow[:, j * BLK:(j + 1) * BLK], bk[j][0:RANK, 0:BLK], ACT.Copy)
            last.then_inc(taken[0], 1)
            for h in range(H):
                act.wait_ge(proj_ready, 2 + h)
                if h >= 2:
                    act.wait_ge(b_spilled[h % 2], 16)
                for j in range(3):
                    last = f(absz[h % 2][:, j * BLK:(j + 1) * BLK], bk[3 * ((1 + h) % 2) + j][:, 0:BLK], ACT.Abs,
                             bias=par[:, 16 + h:17 + h])
                last.then_inc(absz_made, 1)
                act.drain()
                f(absz[h % 2], absz[h % 2], ACT.Exp, scale=-1.0)
                act.drain()
                f(absz[h % 2], absz[h % 2], ACT.Ln, bias=1.0).then_inc(ln_made, 1)
            for n in range(1 + H, 1 + H + CC):
                c = n - 1 - H
                act.wait_ge(proj_ready, n + 1)
                for dst, src in u_parts(c, n):
                    last = f(dst, src, ACT.Sigmoid)
                last.then_inc(taken[n % 2], 1)
            for m in range(2 * H):
                n = 1 + H + 2 * CC + m
                act.wait_ge(proj_ready, n + 1)
                if m >= 2:
                    act.wait_ge(st_spilled[m % 2], 16 * (m // 2))
                for j in range(3):
                    last = f(st[m % 2][:, j * BLK:(j + 1) * BLK], bk[3 * (n % 2) + j][:, 0:BLK], ACT.Copy,
                             scale=float(DK) ** -0.5 if m < H else 1.0)
                last.then_inc(taken[n % 2], 1)
                act.drain().then_inc(qk_staged, 1)
            for b in range(2):
                act.wait_ge(st_spilled[b], 16 * H)
            for m in range(VRJ):
                r = rows(m % NT)
                act.wait_ge(vr_ready, m + 1)
                if m >= 3:
                    act.wait_ge(vr_spilled[m % 3], 16 * (m // 3))
                f(st3[m % 3][0:r, :], bk[m % 6][0:r, :], ACT.Copy if m < VRJ // 2 else ACT.Silu) \
                    .then_inc(vr_staged, 1)
            for b in range(3):
                act.wait_ge(vr_spilled[b], 16 * VRJ // 3)
            act.wait_ge(newc_T, 1)
            f(st3[3][0:PAD, :], bk[6][0:PAD, :], ACT.Copy).then_inc(newc_staged, 1)
            for hf in range(2):
                act.wait_ge(newc_T, 2 + hf)
                f(st3[hf][0:4 * PAD, :], bk[7 - hf][0:4 * PAD, :], ACT.Copy).then_inc(newc_staged, 1)
            for b in range(2):
                act.wait_ge(b_spilled[b], 16 * (H // 2))
            for j in range(3):
                act.wait_ge(centred, j + 1)
                if j == 2:
                    act.wait_ge(var_ready, 1)
                f(sq[j % 2], ybuf[:, :, j * BLK:(j + 1) * BLK], ACT.Square).then_inc(squared, 1)
            for j in range(3):
                act.wait_ge(var_ready, j + 1)
                f(stdb[j], bk[2 * j + 1][:, 0:BLK], ACT.Sqrt, bias=eps_t).then_inc(std_ready, 1)
            for j in range(3):
                act.wait_ge(normed, j + 1)
                for c in range(CC):
                    v = ybuf[:, c, j * BLK:(j + 1) * BLK]
                    last = f(v, v, ACT.Silu, scale=par[:, 24 + c:25 + c], bias=par[:, 28 + c:29 + c])
                last.then_inc(y_ready, 1)
            for b in range(3):
                act.wait_ge(newc_out[b], 16)

            def gate_out(c, k, j):
                g = k * 3 + j
                act.wait_ge(gate_ready, c * 6 + (g + 1))
                if j == 0:
                    act.wait_ge(st_spilled[k], c * 16 + 16 * H)
                settle(act)
                f(st[k][:, j * BLK:(j + 1) * BLK], bk[g % 2][:, 0:BLK], ACT.Identity,
                  bias=par[:, bass.ds(c * 2 + k, 1)]).then_inc(gate_taken, 1)

            INV = 1.0 / GATE_NORM
            with act.Fori(0, NCH // 2) as i:
                for b in range(2):
                    c = act.snap(i * 2 + b)
                    for l in range(LV):
                        act.wait_ge(diff_made, c * (LV + 1) + (l + 1))
                        f(lev[:, l, :], lev[:, l, :], ACT.Exp, scale=INV).then_inc(exp_made, 1)
                        if l in (2, 5):
                            gate_out(c, 0, l // 3)
                    act.wait_ge(diff_made, c * (LV + 1) + (LV + 1))
                    f(ebuf[:, :, :], qkb[b][:, 2, :, :], ACT.Exp, scale=INV).then_inc(exp_made, 1)
                    f(kdT[:, :, :], kdT[:, :, :], ACT.Exp, scale=INV).then_inc(exp_made, 1)
                    gate_out(c, 0, 2)
                    act.wait_ge(o_ready, c + 1)
                    for h in range(H):
                        f(lev[:, h, 0:DV], bk[4 + h // 2][:, DV * (h % 2):DV * (h % 2 + 1)], ACT.Square,
                          accum_out=ss4[:, h:h + 1])
                    act.drain()
                    f(rstd4, ss4, ACT.Sqrt, scale=1.0 / DV, bias=eps_t).then_inc(o_rms, 1)
                    for j in range(3):
                        gate_out(c, 1, j)
            R = S_T
            d0, e0 = NCH * (LV + 1), NCH * (LV + 2)
            for x, l in enumerate((LV - 2, LV - 1)):
                v = lev[:, l, :].rearrange("p (h t) -> p h t", h=H)[:, :, 0:R]
                act.wait_ge(diff_made, d0 + x + 1)
                f(v, v, ACT.Exp, scale=INV).then_inc(exp_made, 1)
            act.wait_ge(diff_made, d0 + 3)
            f(ebuf[:, :, 0:R], qkb[0][:, 2, :, 0:R], ACT.Exp, scale=INV).then_inc(exp_made, 1)
            f(kdT[:, :, 0:R], kdT[:, :, 0:R], ACT.Exp, scale=INV).then_inc(exp_made, 1)
            act.wait_ge(o_ready, NCH + 1)
            for h in range(H):
                f(flat(kdT)[0:R, 0:DV], bk[4 + h][0:R, 0:DV], ACT.Square, accum_out=ss4[0:R, h:h + 1])
                act.drain()
            f(rstd4[0:R, :], ss4[0:R, :], ACT.Sqrt, scale=1.0 / DV, bias=eps_t[0:R, :]).then_inc(o_rms, 1)
            for j in range(KC):
                act.wait_ge(gates_loaded[j % 2], 32 * (j // 2 + 1))
                f(st[j % 2], st[j % 2], ACT.Sigmoid)
                f(ggate[j % 2], ggate[j % 2], ACT.Sigmoid).then_inc(gates_sig, 1)
            for t in range(NT + 1):
                if t < NT:
                    b, r = t % 2, rows(t)
                    act.wait_ge(h_made, t + 1)
                    if t >= 2:
                        act.wait_ge(h_spilled[b], 32 * (t // 2))
                        act.wait_ge(hnT_made, t - 1)
                    f(hn[b][0:r, :], hh[b][0:r, :], ACT.Square, accum_out=ss[b][0:r, :])
                    act.drain()
                    f(rstd[b][0:r, :], ss[b][0:r, :], ACT.Sqrt, scale=1.0 / D, bias=eps_t[0:r, :]) \
                        .then_inc(h_squared, 1)
                if t >= 1:
                    r = rows(t - 1)
                    act.wait_ge(gmax_made, t)
                    f(gexp[0:r, :], gl[0:r, 0:NG], ACT.Exp, bias=ngm[0:r, :], accum_out=gsum[0:r, :]) \
                        .then_inc(gsum_made, 1)
                    act.wait_ge(dtop_made, t)
                    f(etop[0:r, :], dtop[0:r, :], ACT.Exp).then_inc(etop_made, 1)

            def act_expert(n, b, free):
                act.wait_ge(eg_done, n + 1)
                f(sgate, bk[2], ACT.Silu).then_inc(sg_made, 1)
                act.wait_ge(ed_done, n + 1)
                act.wait_ge(yo_free, free)
                f(yo[b][:, 0:512], bk[5], ACT.Copy)
                f(yo[b][:, 512:D], bk[6], ACT.Copy).then_inc(ey_taken, 1)

            with act.Fori(0, NE // 2) as i:
                for b in range(2):
                    act_expert(i * 2 + b, b, i * 2 + (b + 1))
            act.wait_ge(more_stored, 16)
            n_more = act.value_load(more_scr[0:1, 2:3], min_val=0, max_val=MAXX)
            with act.Fori(0, MAXX) as j:
                with act.If(n_more > j):
                    act_expert(j + NE, 0, j + (NE + 2))
                with act.Else():
                    act.nop()
                act.nop()
            for t in range(NT):
                b, r = t % 2, rows(t)
                act.wait_ge(f_sum, t + 1)
                f(f0[b][0:r, :], fh[b][0:r, :], ACT.Square, accum_out=ss[b][0:r, :])
                act.drain()
                f(rstd[b][0:r, :], ss[b][0:r, :], ACT.Sqrt, scale=1.0 / D, bias=eps_t[0:r, :]).then_inc(f_rms, 1)

        @block.vector
        def _(dve):
            def tt(out, x, y, op):
                return dve.tensor_tensor(out, x, y, op)

            def bc(x, n):
                return x.unsqueeze(2).broadcast_to([x.shape[0], x.shape[1], n])

            dve.wait_ge(par_ready, 1)
            dve.tensor_copy(par[:, :], bk[6][:, 0:48])
            dve.tensor_copy(dwT[:, :], bk[6][:, 64:64 + CW * CC])
            dve.drain()
            dve.sem_inc(xn_made, 2)
            dve.sem_inc(nT_made, 2)

            def norm_tile(b, r, t, t0):
                dve.wait_ge(x_rms, t + 1)
                dve.reciprocal(rstd[b][0:r, :], rstd[b][0:r, :])
                dve.drain()
                dve.tensor_scalar(xn[b][0:r, :], xt[b][0:r, :], rstd[b][0:r, :], None, ALU.mult) \
                    .then_inc(xn_made, 1)
                dve.wait_ge(xT_ready, t + 1)
                for q in range(2):
                    last = tt(nT[:, 4 * q:4 * q + 4, t0],
                              bk[2 * b + q].rearrange("p (k t) -> p k t", t=P)[:, :, 0:r],
                              bc(par[:, 40 + 4 * q:44 + 4 * q], r), ALU.mult)
                last.then_inc(nT_made, 1)

            with dve.Fori(0, NCH // 2) as i:
                for b in range(2):
                    norm_tile(b, P, i * 2 + b, bass.ds(i * 256 + b * P, P))
            norm_tile(0, S_T, NCH, slice(SEQ, T))
            for h in range(H):
                n, az = 1 + h, absz[h % 2]
                dve.drain()
                dve.wait_ge(proj_ready, n + 1)
                dve.wait_ge(absz_made, h + 1)
                bias = par[:, 16 + h:17 + h]
                for j in range(3):
                    dve.tensor_scalar(minz[:, j * BLK:(j + 1) * BLK], bk[3 * (n % 2) + j][:, 0:BLK], bias,
                                      0.0, ALU.add, ALU.min)
                dve.drain()
                dve.wait_ge(ln_made, h + 1)
                tt(minz, minz, az, ALU.subtract).then_inc(taken[n % 2], 1)
                dve.drain()
                spans = [(c * P, P) for c in range(NCH)] + [(SEQ + b * NS, NS) for b in range(NB)]
                for t0, n_t in spans:
                    last = dve.tensor_tensor_scan(az[:, t0:t0 + n_t], ones[:, 0:n_t], minz[:, t0:t0 + n_t], 0.0,
                                                  ALU.mult, ALU.add)
                last.then_inc(b_made, 1)
            for c in range(CC):
                n = 1 + H + CC + c
                dve.wait_ge(proj_ready, n + 1)
                dve.wait_ge(taken[n % 2], n // 2)
                for dst, src in u_parts(c, n):
                    last = tt(dst, src, dst, ALU.mult)
                last.then_inc(taken[n % 2], 1)
                dve.drain().then_inc(u_made, 1)
            dve.wait_ge(sc_T, 1)
            us = u[:, :, UP:UW].rearrange("p c (b w) -> p c b w", w=US)
            for hf in range(2):
                for c in range(CC):
                    last = dve.tensor_copy(us[:, c, 4 * hf:4 * hf + 4, 0:PAD],
                                           bk[6 + hf][:, c * 4 * PAD:(c + 1) * 4 * PAD]
                                           .rearrange("p (b w) -> p b w", w=PAD))
            last.then_inc(sc_taken, 1)
            dve.drain()
            dve.wait_ge(u_padded, 1)
            dve.wait_ge(table_filled, 16)
            ysamp = ybuf[:, :, SEQ:T].rearrange("p c (b s) -> p c b s", s=NS)
            for c in range(CC):
                tap, db = dwT[:, c:c + 1], par[:, 20 + c:21 + c]
                dve.tensor_scalar(ybuf[:, c, 0:SEQ], u[:, c, 0:SEQ], tap, db, ALU.mult, ALU.add)
                dve.tensor_scalar(ysamp[:, c], us[:, c, :, 0:NS], tap, db, ALU.mult, ALU.add)
            with dve.Fori(1, CW) as w:
                dve.drain()
                for c in range(CC):
                    tap = dwT[:, bass.ds(w * CC + c, 1)]
                    dve.scalar_tensor_tensor(ybuf[:, c, 0:SEQ], u[:, c, bass.ds(w, SEQ)], tap, ybuf[:, c, 0:SEQ],
                                             ALU.mult, ALU.add)
                    dve.scalar_tensor_tensor(ysamp[:, c], us[:, c, :, bass.ds(w, NS)], tap, ysamp[:, c],
                                             ALU.mult, ALU.add)
            dve.drain().then_inc(conv_made, 1)
            for j in range(3):
                dve.wait_ge(mean_ready, j + 1)
                v = ybuf[:, :, j * BLK:(j + 1) * BLK]
                mean = bk[2 * j][:, 0:BLK].unsqueeze(1).broadcast_to([P, CC, BLK])
                tt(v, v, mean, ALU.subtract).then_inc(centred, 1)
            for j in range(3):
                dve.wait_ge(std_ready, j + 1)
                dve.reciprocal(stdb[j], stdb[j])
                dve.drain()
                v = ybuf[:, :, j * BLK:(j + 1) * BLK]
                tt(v, v, stdb[j].unsqueeze(1).broadcast_to([P, CC, BLK]), ALU.mult).then_inc(normed, 1)

            dve.wait_ge(attn_zero, 1)
            dve.memset(state[:, :, :], 0.0)
            dve.drain().then_inc(s_made, 1)
            dve.sem_inc(lev_taken, 2)

            def halves(x, m, n_t=P):
                v = x.rearrange("p h (n z) -> p (h n) z", z=2 * m) if n_t == P else x
                return v[..., 0:m], v[..., m:2 * m], v[..., m - 1:m]

            def chunk(c, b, i, t0):
                dve.wait_ge(chunk_loaded[b], i * 48 + 48)
                q, k, B = (qkb[b][:, w, :, :] for w in range(3))
                for l in range(LV):
                    m = 64 >> l
                    le, ri = lev_halves(l, m)
                    bl, br_, bm = halves(B, m)
                    mid = bm.broadcast_to([P, H * P // (2 * m), m])
                    tt(ri, br_, mid, ALU.subtract)
                    tt(le, mid, bl, ALU.subtract).then_inc(diff_made, 1)
                tt(kdT[:, :, :], B[:, :, P - 1:P].broadcast_to([P, H, P]), B, ALU.subtract).then_inc(diff_made, 1)
                for l in range(LV):
                    m = 64 >> l
                    le, ri = lev_halves(l, m)
                    dve.wait_ge(exp_made, c * (LV + 2) + (l + 1))
                    tt(ri, ri, halves(q, m)[1], ALU.mult)
                    tt(le, le, halves(k, m)[0], ALU.mult)
                dve.wait_ge(exp_made, c * (LV + 2) + (LV + 2))
                tt(qe[:, :, :], q, ebuf[:, :, :], ALU.mult)
                tt(kdT[:, :, :], kdT[:, :, :], k, ALU.mult).then_inc(prep_made, 1)
                for l in range(LV + 2):
                    x = (LV + 2) * b + l
                    src = bk[2 + x % 2]
                    dve.wait_ge(lev_ready, c * (LV + 2) + (l + 1))
                    settle(dve)
                    take_level(l, src, P)
                dve.wait_ge(ds_ready, c + 1)
                for h in range(H):
                    last = dve.scalar_tensor_tensor(state[:, h, :], state[:, h, :], ebuf[:, h, P - 1:P],
                                                    bk[6 + h // 2][:, DV * (h % 2):DV * (h % 2 + 1)],
                                                    ALU.mult, ALU.add)
                last.then_inc(s_made, 1)
                dve.wait_ge(o_rms, c + 1)
                dve.wait_ge(vrc_loaded[b], i * 32 + 32)
                dve.reciprocal(rstd4, rstd4)
                dve.drain()
                for h in range(H):
                    last = dve.scalar_tensor_tensor(onorm[:, h * DV:(h + 1) * DV],
                                                    bk[4 + h // 2][:, DV * (h % 2):DV * (h % 2 + 1)],
                                                    rstd4[:, h:h + 1], vrbuf[:, b, 1, h * DV:(h + 1) * DV],
                                                    ALU.mult, ALU.mult)
                last.then_inc(on_made, 1)
                take_oT(c + 1, P, t0)

            def take_oT(ready, r, t0):
                dve.wait_ge(oT_ready, ready)
                for q in range(2):
                    last = tt(oT[:, 4 * q:4 * q + 4, t0],
                              bk[4 + q].rearrange("p (k t) -> p k t", t=P)[:, :, 0:r],
                              bc(par[:, 32 + 4 * q:36 + 4 * q], r), ALU.mult)
                last.then_inc(oT_taken, 1)

            def lev_halves(l, m):
                v = lev[:, l, :].rearrange("p (n z) -> p n z", z=2 * m)
                return v[:, :, 0:m], v[:, :, m:2 * m]

            def take_level(l, src, r):
                if l < LV:
                    m, n = 64 >> l, r // (2 * (64 >> l))
                    for h in range(H):
                        dst = attn[0:r, h, 0:r].rearrange("p (n z) -> p n z", z=2 * m)[:, :, m:2 * m]
                        last = dve.copy_predicated(
                            dst, masks[0:r, l * 64:l * 64 + r // 2].rearrange("p (n i) -> p n i", i=m),
                            src[0:r, h * (r // 2):(h + 1) * (r // 2)].rearrange("p (n i) -> p n i", i=m))
                    last.then_inc(lev_taken, 1)
                    dve.drain()
                elif l == LV:
                    for h in range(H):
                        last = dve.copy_predicated(attn[0:r, h, 0:r], masks[0:r, LV * 64:LV * 64 + r],
                                                   src[0:r, h * r:(h + 1) * r])
                    last.then_inc(lev_taken, 1)
                    dve.drain()
                else:
                    dve.tensor_copy(kdn[0:r, :], src[0:r, :]).then_inc(lev_taken, 1)

            with dve.Fori(0, NCH // 2) as i:
                for b in range(2):
                    chunk(dve.snap(i * 2 + b), b, i, bass.ds(i * 256 + b * P, P))
            R = S_T
            e0, l0 = NCH * (LV + 2), NCH * (LV + 2)
            dve.wait_ge(chunk_loaded[0], 48 * (NCH // 2 + 1))
            q, k, B = (qkb[0][:, w, :, 0:R] for w in range(3))

            def samp(x, m):
                v = x.rearrange("p h (n z) -> p h n z", z=2 * m)
                return v[:, :, :, 0:m], v[:, :, :, m:2 * m], v[:, :, :, m - 1:m]

            def samp_lev(l):
                return lev[:, l, :].rearrange("p (h t) -> p h t", h=H)[:, :, 0:R]

            for l in (LV - 2, LV - 1):
                m = 64 >> l
                for h in range(H):
                    le, ri, _ = samp(samp_lev(l)[:, h:h + 1], m)
                    bl, br_, bm = samp(B[:, h:h + 1], m)
                    mid = bm[:, 0].broadcast_to([P, R // (2 * m), m])
                    tt(ri[:, 0], br_[:, 0], mid, ALU.subtract)
                    last = tt(le[:, 0], mid, bl[:, 0], ALU.subtract)
                last.then_inc(diff_made, 1)
            for h in range(H):
                bb = B[:, h, :].rearrange("p (n z) -> p n z", z=NS)
                last = tt(kdT[:, h, 0:R].rearrange("p (n z) -> p n z", z=NS),
                          bb[:, :, NS - 1:NS].broadcast_to([P, NB, NS]), bb, ALU.subtract)
            last.then_inc(diff_made, 1)
            for x, l in enumerate((LV - 2, LV - 1)):
                m = 64 >> l
                dve.wait_ge(exp_made, e0 + x + 1)
                for h in range(H):
                    le, ri, _ = samp(samp_lev(l)[:, h:h + 1], m)
                    ql, qr, _ = samp(q[:, h:h + 1], m)
                    kl, kr, _ = samp(k[:, h:h + 1], m)
                    tt(ri[:, 0], ri[:, 0], qr[:, 0], ALU.mult)
                    tt(le[:, 0], le[:, 0], kl[:, 0], ALU.mult)
            dve.wait_ge(exp_made, e0 + 4)
            tt(qe[:, :, 0:R], q, ebuf[:, :, 0:R], ALU.mult)
            tt(kdT[:, :, 0:R], kdT[:, :, 0:R], k, ALU.mult).then_inc(prep_made, 1)
            dve.memset(attn[0:R, :, 0:R], 0.0)
            dve.memset(flat(gwork)[:, 0:NB * H * R], 0.0)
            dve.drain()
            for b in range(NB):
                last = dve.tensor_copy(lev_qem()[:, b, :, b * NS:(b + 1) * NS], qe[:, :, b * NS:(b + 1) * NS])
            last.then_inc(qem_made, 1)
            for x, l in enumerate((LV - 2, LV - 1, LV, LV + 1)):
                dve.wait_ge(lev_ready, l0 + x + 1)
                take_level(l, bk[2], R)
            dve.drain()
            for b in range(2):
                dve.wait_ge(st_spilled[b], 16 * (H + KC))
            for b in range(NB):
                if b >= 2:
                    dve.wait_ge(sds_ready, b - 1)
                dve.tensor_scalar(lev_kdm()[b % 2][0:R, :], kdn[0:R, :], rowmask[0:R, b:b + 1], None, ALU.mult) \
                    .then_inc(kdm_made, 1)
                if b >= 1:
                    new_state(dve, b - 1)
            new_state(dve, NB - 1)
            dve.wait_ge(o_rms, NCH + 1)
            dve.wait_ge(vrc_loaded[0], 32 * (NCH // 2 + 1))
            dve.reciprocal(rstd4[0:R, :], rstd4[0:R, :])
            dve.drain()
            for h in range(H):
                last = dve.scalar_tensor_tensor(onorm[0:R, h * DV:(h + 1) * DV], bk[4 + h][0:R, 0:DV],
                                                rstd4[0:R, h:h + 1], vrbuf[0:R, 0, 1, h * DV:(h + 1) * DV],
                                                ALU.mult, ALU.mult)
            last.then_inc(on_made, 1)
            take_oT(NCH + 1, R, slice(SEQ, T))

            for j in range(KC):
                dve.wait_ge(gates_sig, j + 1)
                dve.wait_ge(conv_ready, j + 1)
                for q in range(3):
                    t0 = slice(q * BLK, (q + 1) * BLK)
                    last = tt(mixT[:, j, t0], bk[q][:, 0:BLK], st[j % 2][:, t0], ALU.mult)
                last.then_inc(conv_taken, 1)
                dve.wait_ge(gla_ready, j + 1)
                for q in range(3):
                    t0 = slice(q * BLK, (q + 1) * BLK)
                    tt(ggate[j % 2][:, t0], bk[3 + q][:, 0:BLK], ggate[j % 2][:, t0], ALU.mult)
                dve.drain()
                tt(mixT[:, j, :], mixT[:, j, :], ggate[j % 2], ALU.add).then_inc(mix_made, 1)

            dve.wait_ge(small_w, 16 * 5)
            dve.wait_ge(const_ready, 4)
            dve.memset(gl[:, NG:8], -BIG)
            for t in range(NT + 2):
                if t < NT:
                    b, r = t % 2, rows(t)
                    dve.wait_ge(hx_loaded[b], 16 * (t // 2 + 1))
                    dve.wait_ge(h_ready, t + 1)
                    if t >= 2:
                        dve.wait_ge(h_spilled[b], 32 * (t // 2))
                    for hf in range(2):
                        last = tt(hh[b][0:r, 512 * hf:512 * hf + 512], bk[2 * b + hf][0:r, :],
                                  hx[b][0:r, 512 * hf:512 * hf + 512], ALU.add)
                    last.then_inc(h_made, 1)
                    dve.wait_ge(h_squared, t + 1)
                    dve.reciprocal(rstd[b][0:r, :], rstd[b][0:r, :])
                    dve.drain()
                    dve.tensor_scalar(hn[b][0:r, :], hh[b][0:r, :], rstd[b][0:r, :], None, ALU.mult) \
                        .then_inc(hn_made, 1)
                if 1 <= t <= NT:
                    b, r = (t - 1) % 2, rows(t - 1)
                    dve.wait_ge(hT_ready, t)
                    for q in range(2):
                        last = tt(hnT[b][:, 4 * q:4 * q + 4, 0:r],
                                  bk[4 + q].rearrange("p (k t) -> p k t", t=P)[:, :, 0:r],
                                  bc(nffn[:, 4 * q:4 * q + 4], r), ALU.mult)
                    last.then_inc(hnT_made, 1)
                    dve.wait_ge(logit_ready, t)
                    pick(dve, t - 1, r, mpick[b])
                if t >= 2:
                    b, r = t % 2, rows(t - 2)
                    dve.wait_ge(rank_ready, t - 1)
                    dve.tensor_tensor(rk[0:r, :], bk[7][0:r, 0:NE], slot0[0:r, :], ALU.add)
                    dve.drain()
                    for k in range(2):
                        dve.tensor_tensor_reduce((junk, junk2)[k][0:r, :],
                                                 rk[0:r, :], mpick[b][0:r, k, :], 1.0, 0.0, ALU.mult, ALU.add,
                                                 slotf[0:r, k:k + 1])
                    dve.tensor_tensor(macc[0:r, :], macc[0:r, :], mpick[b][0:r, 2, :], ALU.add)
                    dve.drain()
                    dve.tensor_copy(sloti[0:r, t - 2, :], slotf[0:r, :]).then_inc(slot_made, 1)
                    dve.drain()
            dve.wait_ge(count_ready, 1)
            dve.tensor_copy(cnt, bk[7][:, 0:NE])
            dve.wait_ge(lists_loaded, 16)
            dve.tensor_copy(lst_f, lst_i).then_inc(lists_f, 1)
            dve.wait_ge(lists_T, 1)
            dve.tensor_copy(lst_tok, bk[6][:, 0:NE])
            dve.tensor_copy(lst_pair, bk[6][:, P:P + NE])
            dve.drain().then_inc(lists_ready, 1)
            dve.wait_ge(further_iota, 1)
            c3 = cnt[0:16, :].unsqueeze(2).broadcast_to([16, NE, NBX])

            def eb(x):
                return x.rearrange("p (e b) -> p e b", b=NBX)

            tt(eb(m_flag), c3, eb(m_th), ALU.is_gt)
            dve.drain()
            dve.tensor_tensor_scan(m_rank, m_one, m_flag, 0.0, ALU.mult, ALU.add)
            dve.drain()
            dve.tensor_scalar(m_eq, m_rank, jidx[0:16, :], None, ALU.is_equal)
            dve.drain()
            tt(m_eq, m_eq, m_flag, ALU.mult)
            dve.drain()
            dve.tensor_tensor_reduce(m_val, m_eq, m_base, 1.0, 0.0, ALU.mult, ALU.add, m_out[:, 0:1])
            dve.drain()
            dve.tensor_tensor_reduce(m_val, m_eq, m_e, 1.0, 0.0, ALU.mult, ALU.add, m_out[:, 1:2])
            dve.tensor_copy(m_out[:, 2:3], m_rank[:, NF - 1:NF])
            dve.memset(m_out[:, 3:4], 0.0)
            dve.drain()
            dve.tensor_copy(m_int, m_out).then_inc(more_made, 1)

            def take_x(b, ready):
                dve.wait_ge(xgT_ready, ready)
                for q in range(2):
                    last = tt(xeT[b][:, 4 * q:4 * q + 4, :], bk[q].rearrange("p (k t) -> p k t", t=P),
                              bc(nffn[:, 4 * q:4 * q + 4], P), ALU.mult)
                last.then_inc(xeT_made, 1)

            def take_gu(n):
                dve.wait_ge(sg_made, n + 1)
                dve.wait_ge(eu_done, n + 1)
                tt(hid, bk[3], sgate, ALU.mult).then_inc(hid_made, 1)

            def take_hidT(n):
                dve.wait_ge(hidT_ready, n + 1)
                dve.tensor_copy(hidT, bk[4].rearrange("p (k t) -> p k t", t=P)).then_inc(hidT_made, 1)

            take_x(0, 1)
            with dve.Fori(0, NE // 2 - 1) as i:
                for b in range(2):
                    take_gu(i * 2 + b)
                    take_x(1 - b, i * 2 + (b + 2))
                    take_hidT(i * 2 + b)
            take_gu(NE - 2)
            take_x(1, NE)
            take_hidT(NE - 2)
            take_gu(NE - 1)
            take_hidT(NE - 1)
            dve.wait_ge(more_stored, 16)
            n_more = dve.value_load(more_scr[0:1, 2:3], min_val=0, max_val=MAXX)
            with dve.Fori(0, MAXX) as j:
                with dve.If(n_more > j):
                    take_x(0, j + (NE + 1))
                    take_gu(j + NE)
                    take_hidT(j + NE)
                with dve.Else():
                    dve.nop()
                dve.nop()

            def f_add(t):
                b, r = t % 2, rows(t)
                dve.wait_ge(f_loaded[b], 48 * (t // 2 + 1))
                dve.scalar_tensor_tensor(fh[b][0:r, :], f0[b][0:r, :], wts[0:r, t, 0:1], fh[b][0:r, :],
                                         ALU.mult, ALU.add)
                dve.drain()
                dve.scalar_tensor_tensor(fh[b][0:r, :], f1[b][0:r, :], wts[0:r, t, 1:2], fh[b][0:r, :],
                                         ALU.mult, ALU.add).then_inc(f_sum, 1)

            f_add(0)
            dve.wait_ge(nf_loaded, 16)
            for t in range(NT):
                b, r = t % 2, rows(t)
                if t + 1 < NT:
                    f_add(t + 1)
                dve.wait_ge(f_rms, t + 1)
                if t >= 2:
                    dve.wait_ge(f_out[b], 16 * (t // 2))
                dve.reciprocal(rstd[b][0:r, :], rstd[b][0:r, :])
                dve.drain()
                dve.scalar_tensor_tensor(fo[b][0:r, :], fh[b][0:r, :], rstd[b][0:r, :], nfin[0:r, :],
                                         ALU.mult, ALU.mult).then_inc(f_made, 1)


_INS = ["x_prompt", "x_sample", "state_conv", "state_gla", "norm_mix", "w_in", "b_gates", "w_gla_gate_up",
        "b_gla_gate_up", "conv_dw", "conv_db", "conv_ln_g", "conv_ln_b", "w_conv_out", "gla_norm_g", "w_gla_out",
        "w_out", "norm_ffn", "w_router_group", "b_router_group", "w_router_expert", "b_router_expert",
        "w_expert_gate", "w_expert_up", "w_expert_down", "norm_final"]
_OUTS = {"y_prompt": (1, 1024, 1024), "y_sample": (8, 4, 1024), "new_conv_prompt": (1, 1, 30, 512),
         "new_gla_prompt": (1, 1, 4, 128, 256), "new_conv_sample": (1, 8, 30, 512),
         "new_gla_sample": (1, 8, 4, 128, 256)}


def kernel(**inputs):
    import numpy as np
    import concourse.bacc as bacc
    from concourse.bass_utils import run_bass_kernel_spmd as run

    nc = bacc.Bacc("TRN2", target_bir_lowering=False, num_devices=1)
    arrays, a, o = {}, {}, {}
    for name in _INS:
        x = np.ascontiguousarray(inputs[name])
        arrays[f"in_{name}"] = x
        a[name] = nc.dram_tensor(f"in_{name}", x.shape, mybir.dt.from_np(x.dtype), kind="ExternalInput").ap()
    for name, shape in _OUTS.items():
        o[name] = nc.dram_tensor(f"out_{name}", shape, F32, kind="ExternalOutput").ap()
    hybrid_layer(nc, a, o)
    r = run(nc, [arrays], core_ids=[0])
    return tuple(r.results[0][f"out_{name}"] for name in _OUTS)
```

```python
from contextlib import ExitStack

import concourse.bass as bass
from concourse import mybir

F32 = mybir.dt.float32
FR = mybir.dt.float32r
I32 = mybir.dt.int32
U32 = mybir.dt.uint32
I8 = mybir.dt.int8
ALU = mybir.AluOpType
ACT = mybir.ActivationFunctionType

P = 128
BIG = 3.0e38
EPS = 1e-6
GATE_NORM = 16.0
NO_PAIR = 4096


def hybrid_layer(nc, a, o):
    SEQ, D = a["x_prompt"].shape[1:]
    NB, NS = a["x_sample"].shape[:2]
    CW = a["conv_dw"].shape[1]
    DC = a["conv_dw"].shape[2]
    _, _, H, DK, DV = a["state_gla"].shape
    RANK = a["w_gla_gate_up"].shape[1]
    NE, _, DE = a["w_expert_gate"].shape[1:]
    NG = a["w_router_group"].shape[2]
    EG = NE // NG
    QK, VW = H * DK, H * DV
    S_T = NB * NS
    T = SEQ + S_T
    KC = D // P
    CC = DC // P
    FC = DE // P
    NCH = SEQ // P
    NT = NCH + 1
    BLK = T // 3
    LV = 7
    CAP = NT * P
    MAXX = 2 * T // (P + 1)
    NBX = NCH
    PAD = CW - 1
    UP = PAD + SEQ
    US = PAD + NS
    UW = UP + NB * US
    assert D == 1024 and T % 3 == 0 and BLK <= 512 and DK == P and DV == 256 and DE == 512
    C_B, C_Q, C_K = DC, 2 * DC, 2 * DC + QK
    C_V = C_K + QK
    C_R = C_V + VW
    C_A = C_R + VW
    C_G = C_A + RANK

    w_in = a["w_in"][0]
    xs_flat = a["x_sample"].rearrange("b s d -> (b s) d")
    xp_flat = a["x_prompt"][0]

    qkb_scr = nc.dram_tensor("qkb_scr", [3, H, P, T], F32).ap()
    vr_scr = nc.dram_tensor("vr_scr", [2, T, VW], F32).ap()
    gate_scr = nc.dram_tensor("gate_scr", [2 * KC, P, T], F32).ap()
    h_scr = nc.dram_tensor("h_scr", [T, D], F32).ap()
    xn_scr = nc.dram_tensor("xn_scr", [T, D], F32).ap()
    y_scr = nc.dram_tensor("y_scr", [2 * T, D], F32).ap()
    slot_scr = nc.dram_tensor("slot_scr", [NE * CAP, 2], I32).ap()
    more_scr = nc.dram_tensor("more_scr", [16, 4], I32).ap()

    ctx = ExitStack()
    with ctx:
        def sb(name, shape, dt=F32):
            return ctx.enter_context(nc.sbuf_tensor(name, shape, dt))

        def sem(name):
            return ctx.enter_context(nc.semaphore(name))

        SLOT = KC * 512
        ident = sb("ident", [P, P])
        ones = sb("ones", [P, P])
        masks = sb("masks", [P, LV * 64 + P], I8)
        par = sb("par", [P, 48])
        rowmask = sb("rowmask", [P, NB])
        small = sb("small", [P, 96])
        wts = sb("wts", [P, NT, 2])
        macc = sb("macc", [P, NE])
        pay = sb("pay", [P, NT, 2, 2], I32)

        base0 = (nc.sbuf_base + 63) // 64 * 64

        def at(name, offset, shape, dt=F32):
            return nc.alloc_sbuf_tensor_at(name, shape, dt, offset=base0 + offset)

        R16 = 4 * SLOT
        O_UO = 6 * R16
        O_Y = O_UO + 4 * KC * T
        O_VR = O_Y + 4 * CC * T
        O_GW = O_VR + R16
        O_QE = O_GW + R16
        KB2 = 4 * H * P
        O_STATE = O_QE + 4 * KB2
        O_EB = O_STATE + 2 * KB2
        O_ON = O_EB + KB2
        O_ST = O_ON + 2 * KB2
        assert base0 + O_ST + 8 * T <= nc.sbuf_usable_end
        wring = at("wring", 0, [P, 6, SLOT])
        uo = at("uo", O_UO, [P, KC, T])
        ybuf = at("ybuf", O_Y, [P, CC, T])
        vrbuf = at("vrbuf", O_VR, [P, 2, 2, VW])
        gwork = at("gwork", O_GW, [P, SLOT])
        qe = at("qe", O_QE, [P, H, P])
        kdT = at("kdT", O_QE + KB2, [P, H, P])
        kdn = at("kdn", O_QE + 2 * KB2, [P, H * P])
        attn = at("attn", O_QE + 3 * KB2, [P, H, P])
        state = at("state", O_STATE, [P, H, DV])
        ebuf = at("ebuf", O_EB, [P, H, P])
        onorm = at("onorm", O_ON, [P, VW])
        stage = at("stage", O_ST, [P, 2, T])
        wH = [at("wH_gate", O_UO, [P, SLOT], FR), at("wH_up", 3 * R16, [P, SLOT], FR),
              at("wH_down", 5 * R16, [P, SLOT], FR)]
        wL = [at("wL_gate", O_UO + R16, [P, SLOT], FR), at("wL_up", 4 * R16, [P, SLOT], FR),
              at("wL_down", O_VR, [P, SLOT], FR)]
        xeH = at("xeH", O_GW, [P, 2, KC, P], FR)
        xeL = at("xeL", O_GW + R16 // 2, [P, 2, KC, P], FR)
        hidTH = at("hidTH", O_Y + R16 // 2, [P, FC, P], FR)
        hidTL = at("hidTL", O_Y + R16 // 2 + KB2, [P, FC, P], FR)

        def flat(t):
            n = len(t.shape)
            if n == 2:
                return t[:, :]
            if n == 3:
                return t[:, :, :].rearrange("p a b -> p (a b)")
            return t[:, :, :, :].rearrange("p a b c -> p (a b c)")

        wslot = [wring[:, s, :].rearrange("p (k n) -> p k n", n=512) for s in range(6)]
        wide = [wring[:, s, :].rearrange("p (k n) -> p k n", n=D) for s in range(6)]
        w_late = flat(gwork).rearrange("p (k n) -> p k n", n=512)
        high = wring[:, 3:6, :].rearrange("p s n -> p (s n)")
        nT = high[:, 0:KC * T].rearrange("p (k t) -> p k t", t=T)
        mixT = nT
        qkb = [high[:, KC * T + 1536 * b:KC * T + 1536 * (b + 1)].rearrange("p (w h t) -> p w h t", w=3, h=H)
               for b in range(2)]
        ggate = [high[:, KC * T + 1080 * b:KC * T + 1080 * b + T] for b in range(2)]
        gw = [wring[:, 2, 2048 * b:2048 * (b + 1)].rearrange("p (k n) -> p k n", n=256) for b in range(2)]
        xt = [vrbuf[:, 0, b, :] for b in range(2)]
        xn = [vrbuf[:, 1, b, :] for b in range(2)]
        u = flat(uo)[:, 0:CC * UW].rearrange("p (c w) -> p c w", w=UW)
        oT = uo
        lev = flat(gwork)[:, 0:LV * H * P].rearrange("p (l n) -> p l n", l=LV)
        absz = [flat(gwork)[:, T * b:T * (b + 1)] for b in range(2)]
        minz = flat(gwork)[:, 2 * T:3 * T]
        sq = [flat(gwork)[:, CC * BLK * b:CC * BLK * (b + 1)].rearrange("p (c t) -> p c t", c=CC) for b in range(2)]
        st = [stage[:, b, :] for b in range(2)]
        st3 = [flat(stage)[:, 512 * b:512 * (b + 1)] for b in range(4)]
        alow = flat(vrbuf)[0:RANK, 2 * D + 0:2 * D + T]
        wal = flat(attn)[:, 0:KC * RANK].rearrange("p (k n) -> p k n", n=RANK)
        wup = flat(qe)[0:RANK, 0:QK]
        prow = flat(kdn)[0:P, 0:P]
        dwrow = flat(kdn)[0:P, P:2 * P]
        scrow = [flat(state)[:, 0:512], flat(state)[:, 512:1024]]
        newc = flat(onorm)[:, 0:CC * NB * PAD].rearrange("p (c n) -> p c n", c=CC)
        mean_w = gwork[:, 3872:3872 + P]
        dwT = gwork[:, 3 * T:3 * T + CW * CC]
        rp = flat(state)
        wr = rp[:, 0:KC * (NG + NE)].rearrange("p (k n) -> p k n", k=KC)
        br = rp[:, 288:324]
        iota_e, iota_g, slot0, upper = rp[:, 332:364], rp[:, 364:396], rp[:, 396:428], rp[:, 428:556]
        eps_t = small[:, 0:1]
        ss = [small[:, 1:2], small[:, 2:3]]
        rstd = [small[:, 3:4], small[:, 4:5]]
        ss4 = small[:, 5:9]
        rstd4 = small[:, 9:13]
        jidx = small[:, 13:14]

        banks = [ctx.enter_context(nc.psum_tensor(f"bank{i}", [P, 512], F32)) for i in range(8)]
        bk = [t[:, :] for t in banks]

        const_step = sem("const_step")
        const_ready = sem("const_ready")
        waits_carried = sem("waits_carried")
        par_loaded = sem("par_loaded")
        par_ready = sem("par_ready")
        x_loaded = [sem(f"x_loaded{b}") for b in range(2)]
        x_rms = sem("x_rms")
        xn_made = sem("xn_made")
        xT_ready = sem("xT_ready")
        nT_made = sem("nT_made")
        w_loaded = [sem(f"w_loaded{s}") for s in range(3)]
        w_free = [sem(f"w_free{s}") for s in range(3)]
        late_loaded = sem("late_loaded")
        small_w = sem("small_w")
        a_loaded = sem("a_loaded")
        attn_zero = sem("attn_zero")
        proj_ready = sem("proj_ready")
        taken = [sem(f"taken{b}") for b in range(2)]
        absz_made = sem("absz_made")
        ln_made = sem("ln_made")
        b_made = sem("b_made")
        b_spilled = [sem(f"b_spilled{b}") for b in range(2)]
        qk_staged = sem("qk_staged")
        st_spilled = [sem(f"st_spilled{b}") for b in range(2)]
        vr_ready = sem("vr_ready")
        vr_staged = sem("vr_staged")
        vr_spilled = [sem(f"vr_spilled{b}") for b in range(3)]
        u_padded = sem("u_padded")
        sc_loaded = sem("sc_loaded")
        sc_T = sem("sc_T")
        sc_taken = sem("sc_taken")
        u_made = sem("u_made")
        newc_made = sem("newc_made")
        newc_T = sem("newc_T")
        newc_staged = sem("newc_staged")
        newc_out = sem("newc_out")
        conv_made = sem("conv_made")
        mean_ready = sem("mean_ready")
        centred = sem("centred")
        squared = sem("squared")
        var_ready = sem("var_ready")
        std_ready = sem("std_ready")
        normed = sem("normed")
        y_ready = sem("y_ready")
        gw_loaded = [sem(f"gw_loaded{b}") for b in range(2)]
        gw_free = sem("gw_free")
        chunk_loaded = [sem(f"chunk_loaded{b}") for b in range(2)]
        vrc_loaded = [sem(f"vrc_loaded{b}") for b in range(2)]
        diff_made = sem("diff_made")
        exp_made = sem("exp_made")
        prep_made = sem("prep_made")
        lev_ready = sem("lev_ready")
        lev_taken = sem("lev_taken")
        gate_ready = sem("gate_ready")
        gate_taken = sem("gate_taken")
        o_ready = sem("o_ready")
        ds_ready = sem("ds_ready")
        s_made = sem("s_made")
        o_rms = sem("o_rms")
        on_made = sem("on_made")
        oT_ready = sem("oT_ready")
        oT_taken = sem("oT_taken")
        s_out = sem("s_out")
        s0_loaded = [sem(f"s0_loaded{b}") for b in range(2)]
        qem_made = sem("qem_made")
        kdm_made = sem("kdm_made")
        sds_ready = sem("sds_ready")
        snew_made = sem("snew_made")
        snew_out = [sem(f"snew_out{b}") for b in range(2)]
        gates_loaded = [sem(f"gates_loaded{b}") for b in range(2)]
        gates_sig = sem("gates_sig")
        conv_ready = sem("conv_ready")
        conv_taken = sem("conv_taken")
        gla_ready = sem("gla_ready")
        mix_made = sem("mix_made")
        hx_loaded = [sem(f"hx_loaded{b}") for b in range(2)]
        h_ready = sem("h_ready")
        h_made = sem("h_made")
        h_squared = sem("h_squared")
        hn_made = sem("hn_made")
        h_spilled = [sem(f"h_spilled{b}") for b in range(2)]
        hT_ready = sem("hT_ready")
        hnT_made = sem("hnT_made")
        logit_ready = sem("logit_ready")
        gmax_made = sem("gmax_made")
        gsum_made = sem("gsum_made")
        dtop_made = sem("dtop_made")
        etop_made = sem("etop_made")
        pick_made = sem("pick_made")
        rank_ready = sem("rank_ready")
        slot_made = sem("slot_made")
        table_filled = sem("table_filled")
        scattered = sem("scattered")
        count_ready = sem("count_ready")
        more_made = sem("more_made")
        more_stored = sem("more_stored")
        lists_loaded = sem("lists_loaded")
        lists_f = sem("lists_f")
        lists_T = sem("lists_T")
        lists_ready = sem("lists_ready")
        xg_loaded = [sem(f"xg_loaded{b}") for b in range(2)]
        xgT_ready = sem("xgT_ready")
        xeH_made = sem("xeH_made")
        xe_made = sem("xe_made")
        mw_loaded = [sem(f"mw_loaded_{k}") for k in ("gate", "up", "down")]
        wH_made = [sem(f"wH_made_{k}") for k in ("gate", "up", "down")]
        wL_made = [sem(f"wL_made_{k}") for k in ("gate", "up", "down")]
        eg_done = sem("eg_done")
        eu_done = sem("eu_done")
        sg_made = sem("sg_made")
        hid_made = sem("hid_made")
        hidT_ready = sem("hidT_ready")
        hidTH_made = sem("hidTH_made")
        hidT_made = sem("hidT_made")
        ed_done = sem("ed_done")
        ey_taken = sem("ey_taken")
        yo_free = sem("yo_free")
        y_scattered = [sem(f"y_scattered{b}") for b in range(2)]
        more_idx = [sem(f"more_idx{b}") for b in range(2)]
        moe_done = sem("moe_done")
        f_loaded = [sem(f"f_loaded{b}") for b in range(3)]
        f_sum = sem("f_sum")
        f_rms = sem("f_rms")
        f_made = sem("f_made")
        f_out = [sem(f"f_out{b}") for b in range(3)]

        def rows(t):
            return P if t < NCH else S_T

        def x_tile(t):
            return xp_flat[t * P:(t + 1) * P, :] if t < NCH else xs_flat

        NPROJ = 1 + H + 4 * CC
        Z_JOB, B_JOB = (1, 3, 5, 7), (2, 4, 6, 8)
        LN_JOB = (18, 22, 26)
        assert sorted(Z_JOB + B_JOB) == list(range(1, 1 + H + CC))
        VRJ = 4 * NT
        xg = [flat(stage)[:, D * b:D * (b + 1)] for b in range(2)]
        yo = [flat(ybuf)[:, D * b:D * (b + 1)] for b in range(2)]
        sgate = flat(ybuf)[:, 3 * D:3 * D + DE]
        hid = flat(ybuf)[:, 3 * D + DE:4 * D]
        nffn = onorm[:, :]
        hx = [vrbuf[:, 0, b, :] for b in range(2)]
        hh = [vrbuf[:, 1, b, :] for b in range(2)]
        hn = [flat(ybuf)[:, D * b:D * (b + 1)] for b in range(2)]
        hnT = [flat(ybuf)[:, D * (2 + b):D * (3 + b)].rearrange("p (k t) -> p k t", t=P) for b in range(2)]
        rs = flat(kdn)
        gl, gm8, ngm, psel = rs[:, 0:8], rs[:, 8:16], rs[:, 16:17], rs[:, 17:18]
        gif, gsum, dtop, etop = rs[:, 18:19], rs[:, 19:20], rs[:, 20:21], rs[:, 21:22]
        eif, e8 = rs[:, 22:24], rs[:, 24:32]
        el, off, rk, slotf = rs[:, 32:64], rs[:, 64:96], rs[:, 192:224], rs[:, 224:226]
        junk = rs[:, 256:288]
        gexp = rs[:, 288:292]
        mpick = [rs[:, 320 + 96 * b:320 + 96 * (b + 1)].rearrange("p (m e) -> p m e", m=3) for b in range(2)]
        ri = flat(attn).bitcast(U32)
        gi8, ei8 = ri[:, 0:8], ri[:, 8:16]
        sloti = flat(attn).bitcast(I32)[:, 16:16 + 2 * NT].rearrange("p (t k) -> p t k", k=2)
        lst_i = flat(ebuf).bitcast(I32)[0:NE, 0:2 * P]
        lst_f = flat(ebuf)[0:NE, 2 * P:4 * P]
        lst_tok = flat(kdT).bitcast(I32)[:, 0:NE]
        lst_pair = flat(kdT).bitcast(I32)[:, NE:2 * NE]
        col_tok = [flat(kdT).bitcast(I32)[:, 64 + b:65 + b] for b in range(2)]
        col_pair = [flat(kdT).bitcast(I32)[:, 66 + b:67 + b] for b in range(2)]
        more_col = [flat(kdT).bitcast(I32)[:, 68 + 2 * b:70 + 2 * b] for b in range(2)]
        mw = flat(qe)
        NF = NE * NBX
        m_flag, m_rank = mw[0:16, 0:NF], mw[0:16, NF:2 * NF]
        m_eq, m_val = flat(attn)[0:16, 0:NF], flat(attn)[0:16, NF:2 * NF]
        m_base = flat(onorm)[0:16, 0:NF]
        m_e = flat(onorm)[0:16, NF:2 * NF]
        m_th = flat(onorm)[0:16, 2 * NF:3 * NF]
        m_one = flat(onorm)[0:16, 3 * NF:4 * NF]
        m_out = small[0:16, 16:20]
        m_int = small[0:16, 20:24].bitcast(I32)
        cnt = small[:, 32:32 + NE]
        fh = [wring[:, b, 0:D] for b in range(3)]
        f0 = [wring[:, b, D:2 * D] for b in range(3)]
        f1 = [wring[:, b, 2 * D:3 * D] for b in range(3)]
        fo = [wring[:, b, 3 * D:4 * D] for b in range(3)]
        nfin = wring[:, 3, 0:D]

        W_GATE, W_UP, W_DOWN = range(3)
        RAW = (0, 2, 1)
        RAWV = [wring[:, r, :] for r in RAW]
        HALF = SLOT // 2

        def maybe(eng, more, work, other=None):
            if more is None:
                work()
                return
            with eng.If(more):
                work()
            with eng.Else():
                (other or eng.nop)()
            eng.nop()

        def further_blocks(eng, n_more, work):
            with eng.Fori(0, MAXX // 2) as i:
                def two():
                    work(i, 0)
                    maybe(eng, n_more > i * 2 + 1, lambda: work(i, 1))
                maybe(eng, n_more > i * 2, two)

        def settle(eng):
            eng.sem_inc(waits_carried, 1)

        def load_w(sp, kind, e):
            w = a[("w_expert_gate", "w_expert_up", "w_expert_down")[kind]]
            if isinstance(e, int):
                src = w[0, e].rearrange("(p k) n -> p (k n)", p=P)
            else:
                src = w[0, bass.ds(e, 1)].rearrange("e (p k) n -> p (e k n)", p=P)
            sp.dma_start(RAWV[kind], src).then_inc(mw_loaded[kind], 16)

        def lev_qem():
            return flat(gwork)[:, 0:NB * H * S_T].rearrange("p (b h t) -> p b h t", b=NB, h=H)

        def lev_kdm():
            return [flat(gwork)[:, 1024 + 512 * b:1536 + 512 * b] for b in range(2)]

        def new_state(dve, b):
            dve.wait_ge(sds_ready, b + 1)
            if b >= 2:
                dve.wait_ge(snew_out[b % 2], 16 * (b // 2))
            for h in range(H):
                last = dve.scalar_tensor_tensor(
                    st[b % 2][:, h * DV:(h + 1) * DV], vrbuf[:, 1, b % 2, h * DV:(h + 1) * DV],
                    ebuf[:, h, b * NS + NS - 1:b * NS + NS], bk[h // 2][:, DV * (h % 2):DV * (h % 2 + 1)],
                    ALU.mult, ALU.add)
            last.then_inc(snew_made, 1)

        def pick(dve, t, r, mp):
            lg = bk[6]
            dve.tensor_tensor(gl[0:r, 0:NG], lg[0:r, 0:NG], br[0:r, 0:NG], ALU.add)
            dve.tensor_tensor(el[0:r, :], lg[0:r, NG:NG + NE], br[0:r, NG:NG + NE], ALU.add)
            dve.drain()
            dve.max(gm8[0:r, :], gl[0:r, :])
            dve.drain()
            dve.max_index(gi8[0:r, :], gm8[0:r, :], gl[0:r, :])
            dve.tensor_scalar(ngm[0:r, :], gm8[0:r, 0:1], -1.0, None, ALU.mult).then_inc(gmax_made, 1)
            dve.drain()
            dve.tensor_copy(gif[0:r, :], gi8[0:r, 0:1])
            dve.drain()
            dve.tensor_scalar(off[0:r, :], iota_g[0:r, :], gif[0:r, :], -BIG, ALU.not_equal, ALU.mult)
            dve.drain()
            dve.tensor_tensor(el[0:r, :], el[0:r, :], off[0:r, :], ALU.add)
            dve.drain()
            dve.max(e8[0:r, :], el[0:r, :])
            dve.drain()
            dve.tensor_tensor(dtop[0:r, :], e8[0:r, 1:2], e8[0:r, 0:1], ALU.subtract).then_inc(dtop_made, 1)
            dve.max_index(ei8[0:r, :], e8[0:r, :], el[0:r, :])
            dve.drain()
            dve.tensor_copy(eif[0:r, :], ei8[0:r, 0:2])
            dve.drain()
            for k in range(2):
                dve.tensor_scalar(mp[0:r, k, :], iota_e[0:r, :], eif[0:r, k:k + 1], None, ALU.is_equal)
            dve.drain()
            dve.tensor_tensor(mp[0:r, 2, :], mp[0:r, 0, :], mp[0:r, 1, :], ALU.add).then_inc(pick_made, 1)
            dve.wait_ge(gsum_made, t + 1)
            dve.wait_ge(etop_made, t + 1)
            dve.reciprocal(psel[0:r, :], gsum[0:r, :])
            dve.tensor_scalar(sume[0:r, :], etop[0:r, :], 1.0, None, ALU.add)
            dve.drain()
            dve.reciprocal(sume[0:r, :], sume[0:r, :])
            dve.drain()
            dve.tensor_tensor(wts[0:r, t, 0:1], psel[0:r, :], sume[0:r, :], ALU.mult)
            dve.drain()
            dve.tensor_tensor(wts[0:r, t, 1:2], wts[0:r, t, 0:1], etop[0:r, :], ALU.mult)

        sume = rs[:, 292:293]
        junk2 = flat(attn)[:, 64:96]
        stdb = [flat(gwork)[:, 2 * CC * BLK + BLK * j:2 * CC * BLK + BLK * (j + 1)] for j in range(3)]

        def u_parts(c, n):
            b0 = 3 * (n % 2)
            t2 = SEQ - 2 * BLK
            return [(u[:, c, PAD:PAD + BLK], bk[b0][:, 0:BLK]),
                    (u[:, c, PAD + BLK:PAD + 2 * BLK], bk[b0 + 1][:, 0:BLK]),
                    (u[:, c, PAD + 2 * BLK:UP], bk[b0 + 2][:, 0:t2]),
                    (u[:, c, UP:UW].rearrange("p (b w) -> p b w", w=US)[:, :, PAD:US],
                     bk[b0 + 2][:, t2:BLK].rearrange("p (b s) -> p b s", s=NS))]

        block = ctx.enter_context(nc.Block())

        @block.sync
        def _(sp):
            def cols(c0, n=512):
                return w_in[:, c0:c0 + n].rearrange("(k p) n -> p k n", p=P)

            for b in range(2):
                sp.dma_start(xt[b], xp_flat[b * P:(b + 1) * P, :]).then_inc(x_loaded[b], 16)
            sp.dma_start(prow[0:16, :], a["b_gates"][0].rearrange("(r c) -> r c", c=P)).then_inc(par_loaded, 16)
            for r0, nm in ((16, "b_gla_gate_up"), (20, "conv_db"), (24, "conv_ln_g"), (28, "conv_ln_b"),
                           (32, "gla_norm_g"), (40, "norm_mix")):
                v = a[nm][0].rearrange("(r c) -> r c", c=P)
                sp.dma_start(prow[r0:r0 + v.shape[0], :], v).then_inc(par_loaded, 16)
            sp.dma_start(dwrow[0:CW * CC, :], a["conv_dw"][0].rearrange("w (c p) -> (w c) p", p=P)) \
                .then_inc(par_loaded, 16)
            with sp.Fori(1, NCH // 2) as i:
                for b in range(2):
                    sp.wait_ge(xn_made, i * 2 + b + 1)
                    sp.dma_start(xt[b], xp_flat[bass.ds(i * 256 + b * P, P), :]).then_inc(x_loaded[b], 16)
            sp.wait_ge(xn_made, NCH + 1)
            sp.dma_start(xt[0][0:S_T, :], xs_flat).then_inc(x_loaded[0], 16)
            sp.dma_start(wslot[0], cols(C_B)).then_inc(w_loaded[0], 16)
            sp.dma_start(wslot[1], cols(0)).then_inc(w_loaded[1], 16)
            for n, c0 in enumerate((C_Q, C_K, C_V, C_V + 512, C_R, C_R + 512)):
                sp.wait_ge(w_free[n % 2], n // 2 + 1)
                sp.dma_start(wslot[n % 2], cols(c0)).then_inc(w_loaded[n % 2], 16)
            for b in range(2):
                sp.dma_start(gw[b], cols(C_G + 256 * b, 256)).then_inc(gw_loaded[b], 16)
            for b in range(2):
                sp.wait_ge(b_spilled[b], 16 * (H // 2))
                sp.wait_ge(st_spilled[b], 16 * H)

            def load_qkb(b, t0, n):
                for w in range(3):
                    sp.dma_start(qkb[b][:, w, :, 0:n], qkb_scr[w, :, :, t0].rearrange("h p t -> p h t")) \
                      .then_inc(chunk_loaded[b], 16)

            def load_vr(b, t0, n):
                for w in range(2):
                    sp.dma_start(vrbuf[0:n, b, w, :], vr_scr[w, t0, :]).then_inc(vrc_loaded[b], 16)

            sp.wait_ge(proj_ready, Z_JOB[-1] + 1)
            for b in range(2):
                load_qkb(b, slice(b * P, (b + 1) * P), P)
            for b in range(3):
                sp.wait_ge(vr_spilled[b], 16 * VRJ // 3)
            for b in range(2):
                load_vr(b, slice(b * P, (b + 1) * P), P)
            sp.wait_ge(newc_out, 3 * 16)
            sp.wait_ge(w_free[0], 4)
            sp.dma_start(wide[0], a["w_conv_out"][0].rearrange("(k p) n -> p k n", p=P)).then_inc(w_loaded[0], 16)
            sp.wait_ge(w_free[1], 4)
            sp.dma_start(wslot[1], a["w_gla_out"][0][:, 0:512].rearrange("(k p) n -> p k n", p=P)) \
              .then_inc(w_loaded[1], 16)
            with sp.Fori(1, NCH // 2) as i:
                for b in range(2):
                    sp.wait_ge(oT_ready, i * 2 + b - 1)
                    load_qkb(b, bass.ds(i * 256 + b * P, P), P)
                    load_vr(b, bass.ds(i * 256 + b * P, P), P)
                    sp.wait_ge(gw_free, i * 2 + b - 1)
                    sp.dma_start(gw[b], w_in[:, bass.ds(C_G + i * 512 + 256 * b, 256)]
                                 .rearrange("(k p) n -> p k n", p=P)).then_inc(gw_loaded[b], 16)
            sp.wait_ge(oT_ready, NCH - 1)
            load_qkb(0, slice(SEQ, T), S_T)
            load_vr(0, slice(SEQ, T), S_T)
            sp.wait_ge(oT_ready, NCH)
            for b in range(NB):
                if b >= 2:
                    sp.wait_ge(snew_made, b - 1)
                sp.dma_start(vrbuf[:, 1, b % 2, :].rearrange("p (h v) -> p h v", h=H),
                             a["state_gla"][0, b].rearrange("h k v -> k h v")).then_inc(s0_loaded[b % 2], 16)
            sp.wait_ge(gw_free, NCH)
            sp.dma_start(wslot[2], a["w_gla_out"][0][:, 512:D].rearrange("(k p) n -> p k n", p=P)) \
              .then_inc(w_loaded[2], 16)
            for b in range(2):
                sp.wait_ge(st_spilled[b], 16 * (H + KC))
                sp.wait_ge(snew_out[b], 16 * NB // 2)
            sp.wait_ge(on_made, NCH + 1)
            for j in range(KC):
                if j >= 2:
                    sp.wait_ge(mix_made, j - 1)
                sp.dma_start(st[j % 2], gate_scr[j]).then_inc(gates_loaded[j % 2], 16)
                sp.dma_start(ggate[j % 2], gate_scr[KC + j]).then_inc(gates_loaded[j % 2], 16)
                if j == 0:
                    sp.wait_ge(snew_made, NB)
                    sp.dma_start(w_late, a["w_out"][0][:, 0:512].rearrange("(k p) n -> p k n", p=P)) \
                      .then_inc(late_loaded, 16)
                if j == 5:
                    sp.wait_ge(w_free[1], 5)
                    sp.dma_start(wslot[1], a["w_out"][0][:, 512:D].rearrange("(k p) n -> p k n", p=P)) \
                      .then_inc(w_loaded[1], 16)
            for t in range(NT):
                if t >= 2:
                    sp.wait_ge(h_made, t - 1)
                sp.dma_start(hx[t % 2][0:rows(t), :], x_tile(t)).then_inc(hx_loaded[t % 2], 16)
                if t == 0:
                    sp.wait_ge(w_free[0], 5)
                    load_w(sp, W_GATE, 0)
                    sp.wait_ge(w_free[2], 1)
                    load_w(sp, W_UP, 0)
            sp.wait_ge(w_free[1], 6)
            load_w(sp, W_DOWN, 0)
            sp.wait_ge(scattered, 16 * 2 * NT)
            sp.dma_start(lst_i, slot_scr.rearrange("(e s) w -> e s w", e=NE)[:, 0:P, :]
                         .rearrange("e s w -> e (s w)")).then_inc(lists_loaded, 16)
            with sp.Fori(1, NE) as n:
                for kind in (W_GATE, W_UP, W_DOWN):
                    sp.wait_ge(wL_made[kind], n * 2)
                    load_w(sp, kind, n)
            sp.wait_ge(more_stored, 16)
            n_more = sp.value_load(more_scr[0:1, 2:3], min_val=0, max_val=MAXX)
            def further_loads(i, b):
                j = sp.snap(i * 2 + b)
                e = sp.value_load(more_scr[bass.ds(j, 1), 1:2], min_val=0, max_val=NE - 1)
                at_slot = sp.value_load(more_scr[bass.ds(j, 1), 0:1], min_val=0, max_val=NE * CAP - P)
                sp.wait_ge(xg_loaded[b], i * 16 + 8 * NE)
                settle(sp)
                sp.wait_ge(yo_free, j + NE - 1)
                settle(sp)
                sp.dma_start(more_col[b], slot_scr[bass.ds(at_slot, P), :]).then_inc(more_idx[b], 16)
                for kind in (W_GATE, W_UP, W_DOWN):
                    sp.wait_ge(wL_made[kind], j * 2 + 2 * NE)
                    load_w(sp, kind, e)

            further_blocks(sp, n_more, further_loads)
            sp.wait_ge(moe_done, 1)
            for t in range(NT):
                b, r = t % 3, rows(t)
                if t >= 3:
                    sp.wait_ge(f_made, t - 2)
                for part, src in ((fh, h_scr[t * P:t * P + r, :]), (f0, y_scr[t * P:t * P + r, :]),
                                  (f1, y_scr[T + t * P:T + t * P + r, :])):
                    sp.dma_start(part[b][0:r, :], src).then_inc(f_loaded[b], 16)
                if t == 0:
                    sp.dma_start(nfin, a["norm_final"].rearrange("(a n) -> a n", a=1).broadcast_to([P, D])) \
                      .then_inc(lists_loaded, 16)
            for b in range(3):
                sp.wait_ge(f_out[b], 16 * ((NT + 2 - b) // 3))
            sp.wait_ge(s_out, 16)
            sp.wait_ge(newc_out, 3 * 16)

        @block.gpsimd
        def _(pool):
            pool.memset(ident[:, :], 0.0).then_inc(const_step, 1)
            pool.memset(mean_w[:, :], 1.0 / DC).then_inc(const_step, 1)
            pool.memset(ones[:, :], 1.0).then_inc(const_step, 1)
            pool.memset(masks[:, :], 1).then_inc(const_step, 1)
            pool.memset(rowmask[:, :], 1.0).then_inc(const_step, 1)
            pool.memset(eps_t, EPS).then_inc(const_step, 1)
            pool.memset(attn[:, :, :], 0.0).then_inc(const_step, 1)
            pool.wait_ge(const_step, 7)
            pool.dma_start(wal, w_in[:, C_A:C_A + RANK].rearrange("(k p) n -> p k n", p=P)).then_inc(a_loaded, 16)
            pool.dma_start(wup, a["w_gla_gate_up"][0]).then_inc(a_loaded, 16)
            pool.affine_select(out=ident[:, :], in_=ident[:, :], compare_op=ALU.not_equal, fill=1.0, base=0,
                               pattern=[[-1, P]], channel_multiplier=1).then_inc(const_ready, 1)
            pool.drain()
            for l in range(LV):
                m = 64 >> l
                v = masks[:, l * 64:(l + 1) * 64].rearrange("p (n i) -> p n i", i=m)
                pool.affine_select(out=v, in_=v, compare_op=ALU.is_ge, fill=0.0, base=0,
                                   pattern=[[-2 * m, 64 // m], [0, m]], channel_multiplier=1)
                pool.drain()
                pool.affine_select(out=v, in_=v, compare_op=ALU.is_ge, fill=0.0, base=m - 1,
                                   pattern=[[2 * m, 64 // m], [0, m]], channel_multiplier=-1)
                pool.drain()
            dg = masks[:, LV * 64:LV * 64 + P]
            pool.affine_select(out=dg, in_=dg, compare_op=ALU.is_equal, fill=0.0, base=0,
                               pattern=[[-1, P]], channel_multiplier=1)
            pool.affine_select(out=rowmask[:, :], in_=rowmask[:, :], compare_op=ALU.is_ge, fill=0.0, base=0,
                               pattern=[[-NS, NB]], channel_multiplier=1)
            pool.drain()
            pool.affine_select(out=rowmask[:, :], in_=rowmask[:, :], compare_op=ALU.is_ge, fill=0.0, base=NS - 1,
                               pattern=[[NS, NB]], channel_multiplier=-1)
            pool.iota(pay[:, :, :, :], [[P, NT], [0, 2], [0, 2]], base=0, channel_multiplier=1)
            pool.iota(jidx, [[0, 1]], base=1, channel_multiplier=1, allow_small_or_imprecise_dtypes=True)
            pool.memset(macc[:, :], 0.0)
            pool.drain()
            pool.iota(pay[:, :, 1, 1:2], [[P, NT]], base=T, channel_multiplier=1)
            pool.drain().then_inc(const_ready, 1)
            pool.memset(u[:, :, 0:PAD], 0.0).then_inc(u_padded, 1)
            for hf in range(2):
                pool.dma_start(scrow[hf][0:4 * PAD, :], a["state_conv"][0, 4 * hf:4 * hf + 4]
                               .rearrange("b w c -> (b w) c")).then_inc(sc_loaded, 16)
            fill = flat(ybuf).bitcast(I32)[:, 0:NE * CAP * 2 // P].rearrange("p (s w) -> p s w", w=2)
            pool.memset(fill[:, :, 0:1], 0)
            pool.memset(fill[:, :, 1:2], NO_PAIR)
            pool.drain()
            pool.dma_start(slot_scr.rearrange("(p s) w -> p (s w)", p=P), fill.rearrange("p s w -> p (s w)")) \
                .then_inc(table_filled, 16)
            for h in range(H):
                pool.wait_ge(b_made, h + 1)
                pool.dma_start(qkb_scr[2, h], absz[h % 2]).then_inc(b_spilled[h % 2], 16)
            for n in range(2 * H):
                pool.wait_ge(qk_staged, n + 1)
                pool.dma_start(qkb_scr[n // H, n % H], st[n % 2]).then_inc(st_spilled[n % 2], 16)
            pool.wait_ge(proj_ready, 1)
            pool.memset(attn[:, :, :], 0.0).then_inc(attn_zero, 1)
            pool.wait_ge(u_made, CC)
            pool.wait_ge(sc_taken, 1)
            us = u[:, :, UP:UW].rearrange("p c (b w) -> p c b w", w=US)
            for c in range(CC):
                last = pool.tensor_copy(newc[:, c, :].rearrange("p (b w) -> p b w", w=PAD), us[:, c, :, NS:US])
            last.then_inc(newc_made, 1)
            for m in range(VRJ):
                col, t = divmod(m, NT)
                r = rows(t)
                pool.wait_ge(vr_staged, m + 1)
                pool.dma_start(vr_scr[col // 2, t * P:t * P + r, (col % 2) * 512:(col % 2) * 512 + 512],
                               st3[m % 3][0:r, :]).then_inc(vr_spilled[m % 3], 16)
            pool.wait_ge(newc_staged, 1)
            pool.dma_start(o["new_conv_prompt"][0, 0], st3[3][0:PAD, :]).then_inc(newc_out, 16)
            for hf in range(2):
                pool.wait_ge(newc_staged, 2 + hf)
                pool.dma_start(o["new_conv_sample"][0, 4 * hf:4 * hf + 4].rearrange("b w c -> (b w) c"),
                               st3[hf][0:4 * PAD, :]).then_inc(newc_out, 16)
            with pool.Fori(0, NCH) as c:
                for k in range(2):
                    pool.wait_ge(gate_taken, c * 6 + (3 * k + 5))
                    pool.dma_start(gate_scr[bass.ds(c * 2 + k, 1)].rearrange("a p t -> (a p) t"), st[k]) \
                        .then_inc(st_spilled[k], 16)
            pool.wait_ge(s_made, NCH + 1)
            pool.dma_start(o["new_gla_prompt"][0, 0].rearrange("h k v -> k h v"), state[:, :, :]).then_inc(s_out, 16)
            for b in range(NB):
                pool.wait_ge(snew_made, b + 1)
                pool.dma_start(o["new_gla_sample"][0, b].rearrange("h k v -> k h v"),
                               st[b % 2][:, 0:D].rearrange("p (h v) -> p h v", h=H)).then_inc(snew_out[b % 2], 16)
            pool.wait_ge(s_out, 16)
            pool.dma_start(wr[:, :, 0:NG], a["w_router_group"][0].rearrange("(p k) n -> p k n", p=P)) \
                .then_inc(small_w, 16)
            pool.dma_start(wr[:, :, NG:NG + NE], a["w_router_expert"][0].rearrange("(p k) n -> p k n", p=P)) \
                .then_inc(small_w, 16)
            pool.dma_start(br[:, 0:NG], a["b_router_group"].broadcast_to([P, NG])).then_inc(small_w, 16)
            pool.dma_start(br[:, NG:NG + NE], a["b_router_expert"].broadcast_to([P, NE])).then_inc(small_w, 16)
            pool.wait_ge(oT_ready, NCH + 1)
            pool.dma_start(nffn, a["norm_ffn"].broadcast_to([P, D])).then_inc(small_w, 16)
            pool.affine_select(out=upper[:, :], in_=ones[:, :], compare_op=ALU.is_gt, fill=0.0, base=0,
                               pattern=[[1, P]], channel_multiplier=-1).then_inc(const_ready, 1)
            pool.iota(iota_e[:, :], [[1, NE]], base=0, channel_multiplier=0, allow_small_or_imprecise_dtypes=True)
            pool.iota(iota_g[:, :], [[1, NG], [0, EG]], base=0, channel_multiplier=0,
                      allow_small_or_imprecise_dtypes=True)
            pool.iota(slot0[:, :], [[CAP, NE]], base=0, channel_multiplier=0, allow_small_or_imprecise_dtypes=True)
            pool.drain().then_inc(const_ready, 1)
            pool.wait_ge(table_filled, 16)
            for t in range(NT + 2):
                if t < NT:
                    b, r = t % 2, rows(t)
                    pool.wait_ge(h_made, t + 1)
                    pool.dma_start(h_scr[t * P:t * P + r, :], hh[b][0:r, :]).then_inc(h_spilled[b], 16)
                    pool.wait_ge(hn_made, t + 1)
                    pool.dma_start(xn_scr[t * P:t * P + r, :], hn[b][0:r, :]).then_inc(h_spilled[b], 16)
                if t >= 2:
                    r = rows(t - 2)
                    pool.wait_ge(slot_made, t - 1)
                    for k in range(2):
                        pool.indirect_dma_start(
                            out=slot_scr, out_offset=bass.IndirectOffsetOnAxis(ap=sloti[0:r, t - 2, k:k + 1], axis=0),
                            in_=pay[0:r, t - 2, k, :], in_offset=None).then_inc(scattered, 16)
            it = {"channel_multiplier": 0, "allow_small_or_imprecise_dtypes": True}
            pool.iota(m_base, [[CAP, NE], [P, NBX]], base=P, **it)
            pool.iota(m_e, [[1, NE], [0, NBX]], base=0, **it)
            pool.iota(m_th, [[0, NE], [P, NBX]], base=P, **it)
            pool.memset(m_one, 1.0)
            pool.drain().then_inc(const_ready, 1)
            for b in range(2):
                pool.wait_ge(h_spilled[b], 32 * ((NT + 1 - b) // 2))
            pool.wait_ge(lists_ready, 1)
            pool.sem_inc(yo_free, 2)

            def gather(b, tok, turned):
                if turned is not None:
                    pool.wait_ge(xgT_ready, turned)
                    settle(pool)
                pool.tensor_copy(col_tok[b], tok)
                pool.drain()
                pool.indirect_dma_start(out=xg[b], out_offset=None, in_=xn_scr,
                                        in_offset=bass.IndirectOffsetOnAxis(ap=col_tok[b], axis=0)) \
                    .then_inc(xg_loaded[b], 16)

            def scatter(n, b, done):
                pool.wait_ge(ey_taken, n + 2)
                settle(pool)
                pool.indirect_dma_start(out=y_scr, in_=yo[b], in_offset=None,
                                        out_offset=bass.IndirectOffsetOnAxis(ap=col_pair[b], axis=0),
                                        bounds_check=2 * T - 1, oob_is_err=False).then_inc(y_scattered[b], 16)
                pool.wait_ge(y_scattered[b], done)
                settle(pool)

            def next_pairs(b, pair):
                if pair is not None:
                    pool.tensor_copy(col_pair[b], pair)
                    pool.drain()
                pool.sem_inc(yo_free, 1)

            for b in range(2):
                pool.tensor_copy(col_pair[b], lst_pair[:, b:b + 1])
            pool.drain()
            for b in range(2):
                gather(b, lst_tok[:, b:b + 1], None)
            pool.wait_ge(more_made, 1)
            pool.dma_start(more_scr, m_int).then_inc(more_stored, 16)
            with pool.Fori(0, NE // 2 - 1) as i:
                for b in range(2):
                    n2 = pool.snap(i * 2 + (b + 2))
                    gather(b, lst_tok[:, bass.ds(n2, 1)], i * 2 + (b + 1))
                    scatter(i * 2 + b, b, i * 16 + 16)
                    next_pairs(b, lst_pair[:, bass.ds(n2, 1)])
            n_more = pool.value_load(more_scr[0:1, 2:3], min_val=0, max_val=MAXX)

            def step(n, b, done, more, i):
                def first():
                    pool.wait_ge(more_idx[b], i * 16 + 16)
                    settle(pool)
                    gather(b, more_col[b][:, 0:1], n + 1)
                maybe(pool, more, first)
                scatter(n, b, done)
                maybe(pool, more, lambda: next_pairs(b, more_col[b][:, 1:2]), lambda: next_pairs(b, None))

            for b in range(2):
                step(NE - 2 + b, b, 8 * NE, n_more > b, 0)
            further_blocks(pool, n_more, lambda i, b: step(i * 2 + (NE + b), b, i * 16 + (8 * NE + 16),
                                                           n_more > i * 2 + (b + 2), i + 1))
            pool.sem_inc(moe_done, 1)
            for t in range(NT):
                b, r = t % 3, rows(t)
                pool.wait_ge(f_made, t + 1)
                dst = o["y_prompt"][0, t * P:t * P + r, :] if t < NCH else o["y_sample"].rearrange("b s d -> (b s) d")
                pool.dma_start(dst, fo[b][0:r, :]).then_inc(f_out[b], 16)

        @block.tensor
        def _(pe):
            def mm(out, lhsT, rhs, start, stop, **kw):
                return pe.matmul(out, lhsT=lhsT, rhs=rhs, start=start, stop=stop, **kw)

            pe.wait_ge(const_ready, 1)
            pe.wait_ge(par_loaded, 16 * 8)
            pe.transpose(bk[6][:, 0:48], prow[0:48, :], ident[0:48, 0:48])
            pe.transpose(bk[6][:, 64:64 + CW * CC], dwrow[0:CW * CC, :], ident[0:CW * CC, 0:CW * CC]) \
              .then_inc(par_ready, 1)

            def x_transposes(b, r, wait):
                pe.wait_ge(xn_made, wait)
                for k in range(KC):
                    last = pe.transpose(bk[2 * b + k // 4][:, P * (k % 4):P * (k % 4) + r],
                                        xn[b][0:r, k * P:(k + 1) * P], ident[0:r, 0:r])
                last.then_inc(xT_ready, 1)

            with pe.Fori(0, NCH // 2) as i:
                for b in range(2):
                    pe.wait_ge(nT_made, i * 2 + b + 1)
                    x_transposes(b, P, i * 2 + b + 3)
            pe.wait_ge(nT_made, NCH + 1)
            x_transposes(0, S_T, NCH + 3)

            def project(n, lhs, rhs, m, ks):
                if n >= 2:
                    pe.wait_ge(taken[n % 2], n // 2)
                for j in range(3):
                    for k in range(ks):
                        last = mm(bk[3 * (n % 2) + j][0:m, 0:BLK], lhs(k), rhs(k)[:, j * BLK:(j + 1) * BLK],
                                  k == 0, k == ks - 1)
                return last.then_inc(proj_ready, 1)

            pe.wait_ge(nT_made, NT + 2)
            pe.wait_ge(a_loaded, 32)
            project(0, lambda k: wal[:, k, :], lambda k: nT[:, k, :], RANK, KC)
            pe.wait_ge(taken[0], 1)
            for n in range(1, 1 + H + CC):
                if n in Z_JOB:
                    h = Z_JOB.index(n)
                    project(n, lambda k: wup[:, h * DK:(h + 1) * DK], lambda k: alow, P, 1)
                else:
                    j = B_JOB.index(n)
                    if j == 0:
                        pe.wait_ge(w_loaded[0], 16)
                    project(n, lambda k: wslot[0][:, k, j * P:(j + 1) * P], lambda k: nT[:, k, :], P, KC)
            pe.drain().then_inc(w_free[0], 1)
            n = 1 + H + CC
            for s in range(1, 4):
                pe.wait_ge(w_loaded[s % 2], 16 * (s // 2 + 1))
                for j in range(CC):
                    last = project(n, lambda k: wslot[s % 2][:, k, j * P:(j + 1) * P], lambda k: nT[:, k, :], P, KC)
                    n += 1
                pe.drain().then_inc(w_free[s % 2], 1)
                if s == 1:
                    pe.wait_ge(sc_loaded, 32)
                    for hf in range(2):
                        for c in range(CC):
                            last = pe.transpose(bk[6 + hf][:, c * 4 * PAD:(c + 1) * 4 * PAD],
                                                scrow[hf][0:4 * PAD, c * P:(c + 1) * P],
                                                ident[0:4 * PAD, 0:4 * PAD])
                    last.then_inc(sc_T, 1)
            assert n == NPROJ
            for b in range(2):
                pe.wait_ge(taken[b], (NPROJ + 1 - b) // 2)
            for m in range(VRJ):
                col, t = divmod(m, NT)
                r = rows(t)
                if t == 0:
                    pe.wait_ge(w_loaded[col % 2], 16 * (col // 2 + 3))
                if m >= 6:
                    pe.wait_ge(vr_staged, m - 5)
                for k in range(KC):
                    last = mm(bk[m % 6][0:r, :], nT[:, k, t * P:t * P + r], wslot[col % 2][:, k, :],
                              k == 0, k == KC - 1)
                last.then_inc(vr_ready, 1)
                if t == NT - 1:
                    pe.drain().then_inc(w_free[col % 2], 1)
                if m in LN_JOB:
                    j = LN_JOB.index(m)
                    if j == 0:
                        pe.wait_ge(sc_taken, 1)
                        pe.wait_ge(conv_made, 1)
                    else:
                        pe.wait_ge(centred, j)
                    for c in range(CC):
                        last = mm(bk[6][:, 0:BLK], mean_w[:, :], ybuf[:, c, j * BLK:(j + 1) * BLK],
                                  c == 0, c == CC - 1)
                    last.then_inc(mean_ready, 1)
                if m - 1 in LN_JOB:
                    j = LN_JOB.index(m - 1)
                    pe.wait_ge(squared, j + 1)
                    if j:
                        pe.wait_ge(std_ready, j)
                    for c in range(CC):
                        last = mm(bk[7][:, 0:BLK], mean_w[:, :], sq[j % 2][:, c, :], c == 0, c == CC - 1)
                    last.then_inc(var_ready, 1)
            pe.wait_ge(newc_made, 1)
            pe.wait_ge(centred, 3)
            pe.wait_ge(std_ready, 3)
            pe.wait_ge(vr_staged, VRJ)
            for c in range(CC):
                last = pe.transpose(bk[6][0:PAD, c * P:(c + 1) * P], u[:, c, UP - PAD:UP], ident[:, :])
            last.then_inc(newc_T, 1)
            for hf in range(2):
                for c in range(CC):
                    last = pe.transpose(bk[7 - 2 * hf][0:4 * PAD, c * P:(c + 1) * P],
                                        newc[:, c, 4 * PAD * hf:4 * PAD * (hf + 1)], ident[:, :])
                last.then_inc(newc_T, 1)

            def gate_block(c, b, k, j, parts=range(KC)):
                g = k * 3 + j
                if parts[0] == 0:
                    pe.wait_ge(gate_taken, c * 6 + (g + 1))
                for q in parts:
                    last = mm(bk[g % 2][:, 0:BLK], gw[b][:, q, k * P:(k + 1) * P],
                              nT[:, q, j * BLK:(j + 1) * BLK], q == 0, q == KC - 1)
                if parts[-1] == KC - 1:
                    last.then_inc(gate_ready, 1)

            def chunk(c, b, i):
                pe.wait_ge(gw_loaded[b], i * 16 + 16)
                for j in range(3):
                    gate_block(c, b, 0, j)
                pe.wait_ge(prep_made, c + 1)
                lv = lev.rearrange("p l (h t) -> p l h t", h=H)
                for l in range(LV + 2):
                    x = (LV + 2) * b + l
                    pe.wait_ge(lev_taken, c * (LV + 2) + (l + 1))
                    dst = bk[2 + x % 2]
                    for h in range(H):
                        if l < LV:
                            m = 64 >> l
                            right = lv[:, l, h, :].rearrange("p (n z i) -> p n z i", z=2, i=m)[:, :, 1, :]
                            last = mm(dst[:, 64 * h:64 * h + 64].rearrange("p (n i) -> p n i", i=m),
                                      lv[:, l, h, :], right, True, True)
                        elif l == LV:
                            last = mm(dst[:, P * h:P * h + P], qkb[b][:, 1, h, :], qkb[b][:, 0, h, :], True, True)
                        else:
                            last = pe.transpose(dst[:, P * h:P * h + P], kdT[:, h, :], ident[:, :])
                    last.then_inc(lev_ready, 1)
                    if l < KC:
                        gate_block(c, b, 1, 0, [l])
                pe.wait_ge(oT_taken, c + 1)
                pe.wait_ge(lev_taken, c * (LV + 2) + (LV + 4))
                pe.wait_ge(s_made, c + 1)
                pe.wait_ge(vrc_loaded[b], i * 32 + 32)
                for h in range(H):
                    dst = bk[4 + h // 2][:, DV * (h % 2):DV * (h % 2 + 1)]
                    mm(dst, attn[:, h, :], vrbuf[:, b, 0, h * DV:(h + 1) * DV], True, False)
                    last = mm(dst, qe[:, h, :], state[:, h, :], False, True)
                last.then_inc(o_ready, 1)
                for h in range(H):
                    last = mm(bk[6 + h // 2][:, DV * (h % 2):DV * (h % 2 + 1)], kdn[:, h * P:(h + 1) * P],
                              vrbuf[:, b, 0, h * DV:(h + 1) * DV], True, True)
                last.then_inc(ds_ready, 1)
                for j in range(1, 3):
                    gate_block(c, b, 1, j)
                pe.drain().then_inc(gw_free, 1)
                o_transposes(P, c + 1)

            def o_transposes(r, wait):
                pe.wait_ge(on_made, wait)
                for k in range(KC):
                    last = pe.transpose(bk[4 + k // 4][:, P * (k % 4):P * (k % 4) + r],
                                        onorm[0:r, k * P:(k + 1) * P], ident[0:r, 0:r])
                last.then_inc(oT_ready, 1)

            with pe.Fori(0, NCH // 2) as i:
                for b in range(2):
                    chunk(i * 2 + b, b, i)
            NL = NCH * (LV + 2)
            R = S_T
            pe.wait_ge(prep_made, NCH + 1)
            for x, l in enumerate((LV - 2, LV - 1, LV)):
                m = max(64 >> l, 1)
                if x >= 1:
                    pe.wait_ge(lev_taken, NL + 2 + x)
                for h in range(H):
                    if l < LV:
                        w = lev.rearrange("p l (h t) -> p l h t", h=H)[:, l, h, 0:R]
                        right = w.rearrange("p (n z i) -> p n z i", z=2, i=m)[:, :, 1, :]
                        last = mm(bk[2][0:R, 16 * h:16 * h + 16].rearrange("p (n i) -> p n i", i=m), w, right,
                                  True, True)
                    else:
                        last = mm(bk[2][0:R, R * h:R * h + R], qkb[0][:, 1, h, 0:R], qkb[0][:, 0, h, 0:R],
                                  True, True)
                last.then_inc(lev_ready, 1)
            pe.wait_ge(lev_taken, NL + 2 + 3)
            for h in range(H):
                last = pe.transpose(bk[2][0:R, P * h:P * h + P], kdT[:, h, 0:R], ident[:, :])
            last.then_inc(lev_ready, 1)
            pe.wait_ge(lev_taken, NL + 2 + 4)
            pe.wait_ge(gate_taken, 2 + 6 * NCH)
            pe.wait_ge(vrc_loaded[0], 32 * (NCH // 2 + 1))
            pe.wait_ge(s_made, 1 + NCH)
            pe.wait_ge(oT_taken, 1 + NCH)
            for h in range(H):
                mm(bk[4 + h][0:R, 0:DV], attn[0:R, h, 0:R], vrbuf[0:R, 0, 0, h * DV:(h + 1) * DV], True, False,
                   skip_group_check=True)
            pe.wait_ge(qem_made, 1)
            qem = lev_qem()
            kdm = lev_kdm()
            for b in range(NB):
                pe.wait_ge(s0_loaded[b % 2], 16 * (b // 2 + 1))
                s0 = vrbuf[:, 1, b % 2, :].rearrange("p (h v) -> p h v", h=H)
                for h in range(H):
                    last = mm(bk[4 + h][0:R, 0:DV], qem[:, b, h, :], s0[:, h, :], False, b == NB - 1,
                              skip_group_check=True)
                if b == NB - 1:
                    last.then_inc(o_ready, 1)
                pe.wait_ge(kdm_made, b + 1)
                if b >= 1:
                    pe.wait_ge(snew_made, b)
                for h in range(H):
                    last = mm(bk[h // 2][:, DV * (h % 2):DV * (h % 2 + 1)], kdm[b % 2][0:R, h * P:(h + 1) * P],
                              vrbuf[0:R, 0, 0, h * DV:(h + 1) * DV], True, True)
                last.then_inc(sds_ready, 1)

            pe.wait_ge(snew_made, NB)
            pe.wait_ge(y_ready, 3)
            pe.wait_ge(w_loaded[0], 16 * 5)
            for j in range(KC):
                if j:
                    pe.wait_ge(conv_taken, j)
                for q in range(3):
                    for k in range(CC):
                        last = mm(bk[q][:, 0:BLK], wide[0][:, k, j * P:(j + 1) * P],
                                  ybuf[:, k, q * BLK:(q + 1) * BLK], k == 0, k == CC - 1)
                last.then_inc(conv_ready, 1)
                if j:
                    pe.wait_ge(mix_made, j)
                if j == 0:
                    o_transposes(R, NCH + 1)
                    pe.wait_ge(oT_taken, NCH + 2)
                    pe.wait_ge(w_loaded[1], 16 * 5)
                if j == 4:
                    pe.drain().then_inc(w_free[1], 1)
                    pe.wait_ge(w_loaded[2], 16)
                for q in range(3):
                    for k in range(KC):
                        last = mm(bk[3 + q][:, 0:BLK], wslot[1 + j // 4][:, k, (j % 4) * P:(j % 4 + 1) * P],
                                  oT[:, k, q * BLK:(q + 1) * BLK], k == 0, k == KC - 1)
                last.then_inc(gla_ready, 1)
            pe.drain().then_inc(w_free[2], 1)
            pe.drain().then_inc(w_free[0], 1)

            pe.wait_ge(mix_made, KC)
            pe.wait_ge(late_loaded, 16)
            pe.wait_ge(w_loaded[1], 16 * 6)
            pe.wait_ge(small_w, 16 * 5)
            pe.wait_ge(const_ready, 4)
            def h_half(t, hf):
                for k in range(KC):
                    last = mm(bk[2 * (t % 2) + hf][0:rows(t), :], mixT[:, k, t * P:t * P + rows(t)],
                              (w_late, wslot[1])[hf][:, k, :], k == 0, k == KC - 1)
                return last

            for t in range(NT + 2):
                if t < NT:
                    if t >= 2:
                        pe.wait_ge(h_made, t - 1)
                    h_half(t, 0)
                if 1 <= t <= NT:
                    b, r = (t - 1) % 2, rows(t - 1)
                    pe.wait_ge(hn_made, t)
                    if t >= 2:
                        pe.wait_ge(hnT_made, t - 1)
                    for k in range(KC):
                        last = pe.transpose(bk[4 + k // 4][:, P * (k % 4):P * (k % 4) + r],
                                            hn[b][0:r, k:D:KC], ident[0:r, 0:r])
                    last.then_inc(hT_ready, 1)
                if t < NT:
                    h_half(t, 1).then_inc(h_ready, 1)
                    if t == NT - 1:
                        pe.drain().then_inc(w_free[1], 1)
                if 1 <= t <= NT:
                    b, r = (t - 1) % 2, rows(t - 1)
                    pe.wait_ge(hnT_made, t)
                    if t >= 2:
                        pe.wait_ge(pick_made, t - 1)
                    for k in range(KC):
                        last = mm(bk[6][0:r, 0:NG + NE], hnT[b][:, k, 0:r], wr[:, k, :], k == 0, k == KC - 1)
                    last.then_inc(logit_ready, 1)
                if t >= 2:
                    b, r = t % 2, rows(t - 2)
                    pe.wait_ge(pick_made, t - 1)
                    if t >= 3:
                        pe.wait_ge(slot_made, t - 2)
                    mm(bk[7][0:r, 0:NE], upper[0:r, 0:r], mpick[b][0:r, 2, :], True, False)
                    last = mm(bk[7][0:r, 0:NE], ones[:, 0:r], macc[:, :], False, True)
                    last.then_inc(rank_ready, 1)
            pe.wait_ge(slot_made, NT)
            mm(bk[7][:, 0:NE], ones[:, 0:P], macc[:, :], True, True).then_inc(count_ready, 1)
            pe.wait_ge(lists_f, 1)
            lf = lst_f.rearrange("e (s w) -> e s w", w=2)
            for w in range(2):
                last = pe.transpose(bk[6][:, P * w:P * w + NE], lf[:, :, w], ident[0:NE, 0:NE])
            last.then_inc(lists_T, 1)

            def x_block(b, landed):
                pe.wait_ge(xg_loaded[b], landed)
                for k in range(KC):
                    last = pe.transpose(bk[k // 4][:, P * (k % 4):P * (k % 4 + 1)], xg[b][:, k:D:KC], ident[:, :])
                last.then_inc(xgT_ready, 1)

            def mm3(out, left, right, first, stop):
                (lh, ll), (rh, rl) = left, right
                mm(out, lh, rh, first, False)
                mm(out, lh, rl, False, False)
                return mm(out, ll, rh, False, stop)

            def block_products(n, b, nxt, more):
                pe.wait_ge(xe_made, n + 1)
                for kind, bank, done in ((W_GATE, bk[2], eg_done), (W_UP, bk[3], eu_done)):
                    pe.wait_ge(wL_made[kind], n * 2 + 2)
                    wh, wl = (x[kind][:, :].rearrange("p (k n) -> p k n", k=KC) for x in (wH, wL))
                    for k in range(KC):
                        last = mm3(bank, (xeH[:, b, k, :], xeL[:, b, k, :]), (wh[:, k, :], wl[:, k, :]),
                                   k == 0, k == KC - 1)
                    last.then_inc(done, 1)
                if nxt is not None:
                    maybe(pe, more, lambda: x_block(1 - b, nxt))
                pe.wait_ge(hid_made, n + 1)
                for k in range(FC):
                    last = pe.transpose(bk[4][:, P * k:P * (k + 1)], hid[:, k:DE:FC], ident[:, :])
                last.then_inc(hidT_ready, 1)
                pe.wait_ge(wL_made[W_DOWN], n * 2 + 2)
                pe.wait_ge(ey_taken, n + 1)
                pe.wait_ge(hidT_made, n + 1)
                wh, wl = (x[W_DOWN][:, :].rearrange("p (k n) -> p k n", k=FC) for x in (wH, wL))
                for hf in range(2):
                    cs = slice(hf * 512, (hf + 1) * 512)
                    for k in range(FC):
                        last = mm3(bk[5 + hf], (hidTH[:, k, :], hidTL[:, k, :]), (wh[:, k, cs], wl[:, k, cs]),
                                   k == 0, k == FC - 1)
                last.then_inc(ed_done, 1)

            pe.wait_ge(lists_ready, 1)
            x_block(0, 16)
            with pe.Fori(0, NE // 2 - 1) as i:
                block_products(i * 2, 0, i * 16 + 16, None)
                block_products(i * 2 + 1, 1, i * 16 + 32, None)
            block_products(NE - 2, 0, 8 * NE, None)
            pe.wait_ge(more_stored, 16)
            n_more = pe.value_load(more_scr[0:1, 2:3], min_val=0, max_val=MAXX)
            block_products(NE - 1, 1, 8 * NE + 16, n_more > 0)
            further_blocks(pe, n_more, lambda i, b: block_products(
                i * 2 + (NE + b), b, i * 16 + (8 * NE + 16 + 16 * b), n_more > i * 2 + (b + 1)))

        @block.scalar
        def _(act):
            def f(out, in_, func, **kw):
                return act.activation(out, in_, func, **kw)

            act.wait_ge(const_step, 7)
            act.sem_inc(gate_taken, 2)
            act.sem_inc(ey_taken, 1)

            def rms_tile(b, r, i2, loaded):
                act.wait_ge(x_loaded[b], loaded)
                act.wait_ge(nT_made, i2 + 1)
                f(xn[b][0:r, :], xt[b][0:r, :], ACT.Square, accum_out=ss[b][0:r, :])
                act.drain()
                f(rstd[b][0:r, :], ss[b][0:r, :], ACT.Sqrt, scale=1.0 / D, bias=eps_t[0:r, :]).then_inc(x_rms, 1)

            for t in range(NT):
                rms_tile(t % 2, rows(t), t, t // 2 * 16 + 16)
            act.wait_ge(proj_ready, 1)
            for j in range(3):
                last = f(alow[:, j * BLK:(j + 1) * BLK], bk[j][0:RANK, 0:BLK], ACT.Copy)
            last.then_inc(taken[0], 1)
            for n in range(1, 1 + H + CC):
                act.wait_ge(proj_ready, n + 1)
                if n in B_JOB:
                    for dst, src in u_parts(B_JOB.index(n), n):
                        last = f(dst, src, ACT.Sigmoid)
                    last.then_inc(taken[n % 2], 1)
                    continue
                h = Z_JOB.index(n)
                if h >= 2:
                    act.wait_ge(b_spilled[h % 2], 16)
                for j in range(3):
                    last = f(absz[h % 2][:, j * BLK:(j + 1) * BLK], bk[3 * (n % 2) + j][:, 0:BLK], ACT.Abs,
                             bias=par[:, 16 + h:17 + h])
                last.then_inc(absz_made, 1)
                act.drain()
                f(absz[h % 2], absz[h % 2], ACT.Exp, scale=-1.0)
                act.drain()
                f(absz[h % 2], absz[h % 2], ACT.Ln, bias=1.0).then_inc(ln_made, 1)
            for m in range(2 * H):
                n = 1 + H + 2 * CC + m
                act.wait_ge(proj_ready, n + 1)
                if m >= 2:
                    act.wait_ge(st_spilled[m % 2], 16 * (m // 2))
                for j in range(3):
                    last = f(st[m % 2][:, j * BLK:(j + 1) * BLK], bk[3 * (n % 2) + j][:, 0:BLK], ACT.Copy,
                             scale=float(DK) ** -0.5 if m < H else 1.0)
                last.then_inc(taken[n % 2], 1)
                act.drain().then_inc(qk_staged, 1)
            INV = 1.0 / GATE_NORM

            def factors(c, b, gate):
                for l in range(LV):
                    act.wait_ge(diff_made, c * (LV + 1) + (l + 1))
                    f(lev[:, l, :], lev[:, l, :], ACT.Exp, scale=INV).then_inc(exp_made, 1)
                    if l in (2, 5):
                        gate(l // 3)
                act.wait_ge(diff_made, c * (LV + 1) + (LV + 1))
                f(ebuf[:, :, :], qkb[b][:, 2, :, :], ACT.Exp, scale=INV).then_inc(exp_made, 1)
                f(kdT[:, :, :], kdT[:, :, :], ACT.Exp, scale=INV).then_inc(exp_made, 1)

            for b in range(2):
                act.wait_ge(st_spilled[b], 16 * H)
                act.wait_ge(b_spilled[b], 16 * (H // 2))
            for m in range(VRJ):
                r = rows(m % NT)
                act.wait_ge(vr_ready, m + 1)
                if m >= 3:
                    act.wait_ge(vr_spilled[m % 3], 16 * (m // 3))
                f(st3[m % 3][0:r, :], bk[m % 6][0:r, :], ACT.Copy if m < VRJ // 2 else ACT.Silu) \
                    .then_inc(vr_staged, 1)
                if m in LN_JOB:
                    j = LN_JOB.index(m)
                    act.wait_ge(centred, j + 1)
                    f(sq[j % 2], ybuf[:, :, j * BLK:(j + 1) * BLK], ACT.Square).then_inc(squared, 1)
                if m - 1 in LN_JOB:
                    act.wait_ge(var_ready, LN_JOB.index(m - 1) + 1)
                    f(stdb[LN_JOB.index(m - 1)], bk[7][:, 0:BLK], ACT.Sqrt, bias=eps_t).then_inc(std_ready, 1)
                if m - 2 in LN_JOB:
                    j = LN_JOB.index(m - 2)
                    act.wait_ge(normed, j + 1)
                    for c in range(CC):
                        v = ybuf[:, c, j * BLK:(j + 1) * BLK]
                        last = f(v, v, ACT.Silu, scale=par[:, 24 + c:25 + c], bias=par[:, 28 + c:29 + c])
                    last.then_inc(y_ready, 1)
            factors(0, 0, lambda j: None)
            for b in range(3):
                act.wait_ge(vr_spilled[b], 16 * VRJ // 3)
            act.wait_ge(newc_T, 1)
            f(st3[3][0:PAD, :], bk[6][0:PAD, :], ACT.Copy).then_inc(newc_staged, 1)
            for hf in range(2):
                act.wait_ge(newc_T, 2 + hf)
                f(st3[hf][0:4 * PAD, :], bk[7 - 2 * hf][0:4 * PAD, :], ACT.Copy).then_inc(newc_staged, 1)
            act.wait_ge(newc_out, 3 * 16)

            def gate_out(c, k, j):
                g = k * 3 + j
                act.wait_ge(gate_ready, c * 6 + (g + 1))
                if j == 0:
                    act.wait_ge(st_spilled[k], c * 16 + 16 * H)
                settle(act)
                f(st[k][:, j * BLK:(j + 1) * BLK], bk[g % 2][:, 0:BLK], ACT.Identity,
                  bias=par[:, bass.ds(c * 2 + k, 1)]).then_inc(gate_taken, 1)

            def act_chunk(c, b, nxt):
                for j in range(3):
                    gate_out(c, 0, j)
                act.wait_ge(o_ready, c + 1)
                for h in range(H):
                    f(lev[:, h, 0:DV], bk[4 + h // 2][:, DV * (h % 2):DV * (h % 2 + 1)], ACT.Square,
                      accum_out=ss4[:, h:h + 1])
                act.drain()
                f(rstd4, ss4, ACT.Sqrt, scale=1.0 / DV, bias=eps_t).then_inc(o_rms, 1)
                gate_out(c, 1, 0)
                if nxt:
                    factors(c + 1, 1 - b, lambda j: gate_out(c, 1, 1 + j))
                else:
                    for j in range(1, 3):
                        gate_out(c, 1, j)

            with act.Fori(0, NCH // 2 - 1) as i:
                for b in range(2):
                    act_chunk(act.snap(i * 2 + b), b, True)
            for b in range(2):
                act_chunk(NCH - 2 + b, b, b == 0)
            R = S_T
            d0, e0 = NCH * (LV + 1), NCH * (LV + 2)
            for x, l in enumerate((LV - 2, LV - 1)):
                v = lev[:, l, :].rearrange("p (h t) -> p h t", h=H)[:, :, 0:R]
                act.wait_ge(diff_made, d0 + x + 1)
                f(v, v, ACT.Exp, scale=INV).then_inc(exp_made, 1)
            act.wait_ge(diff_made, d0 + 3)
            f(ebuf[:, :, 0:R], qkb[0][:, 2, :, 0:R], ACT.Exp, scale=INV).then_inc(exp_made, 1)
            f(kdT[:, :, 0:R], kdT[:, :, 0:R], ACT.Exp, scale=INV).then_inc(exp_made, 1)
            act.wait_ge(o_ready, NCH + 1)
            for h in range(H):
                f(flat(kdT)[0:R, 0:DV], bk[4 + h][0:R, 0:DV], ACT.Square, accum_out=ss4[0:R, h:h + 1])
                act.drain()
            f(rstd4[0:R, :], ss4[0:R, :], ACT.Sqrt, scale=1.0 / DV, bias=eps_t[0:R, :]).then_inc(o_rms, 1)
            for j in range(KC):
                act.wait_ge(gates_loaded[j % 2], 32 * (j // 2 + 1))
                f(st[j % 2], st[j % 2], ACT.Sigmoid)
                f(ggate[j % 2], ggate[j % 2], ACT.Sigmoid).then_inc(gates_sig, 1)
            for t in range(NT + 1):
                if t < NT:
                    b, r = t % 2, rows(t)
                    act.wait_ge(h_made, t + 1)
                    if t >= 2:
                        act.wait_ge(h_spilled[b], 32 * (t // 2))
                        act.wait_ge(hnT_made, t - 1)
                    f(hn[b][0:r, :], hh[b][0:r, :], ACT.Square, accum_out=ss[b][0:r, :])
                    act.drain()
                    f(rstd[b][0:r, :], ss[b][0:r, :], ACT.Sqrt, scale=1.0 / D, bias=eps_t[0:r, :]) \
                        .then_inc(h_squared, 1)
                if t >= 1:
                    r = rows(t - 1)
                    act.wait_ge(gmax_made, t)
                    f(gexp[0:r, :], gl[0:r, 0:NG], ACT.Exp, bias=ngm[0:r, :], accum_out=gsum[0:r, :]) \
                        .then_inc(gsum_made, 1)
                    act.wait_ge(dtop_made, t)
                    f(etop[0:r, :], dtop[0:r, :], ACT.Exp).then_inc(etop_made, 1)

            def weight_high(kind, n):
                act.wait_ge(mw_loaded[kind], n * 16 + 16)
                for hf in range(2):
                    cs = slice(hf * HALF, (hf + 1) * HALF)
                    f(wH[kind][:, cs], RAWV[kind][:, cs], ACT.Copy).then_inc(wH_made[kind], 1)

            def x_high(n, b):
                act.wait_ge(xgT_ready, n + 1)
                for q in range(2):
                    last = f(xeH[:, b, 4 * q:4 * q + 4, :].rearrange("p k t -> p (k t)"), bk[q], ACT.Copy)
                last.then_inc(xeH_made, 1)

            def act_block(n, b, free, nxt, more):
                act.wait_ge(eg_done, n + 1)
                f(sgate, bk[2], ACT.Silu).then_inc(sg_made, 1)
                if nxt:
                    maybe(act, more, lambda: weight_high(W_GATE, n + 1))
                act.wait_ge(hidT_ready, n + 1)
                f(hidTH[:, :, :].rearrange("p k t -> p (k t)"), bk[4], ACT.Copy).then_inc(hidTH_made, 1)
                if nxt:
                    def work():
                        x_high(n + 1, 1 - b)
                        weight_high(W_UP, n + 1)
                    maybe(act, more, work)
                act.wait_ge(ed_done, n + 1)
                act.wait_ge(yo_free, free)
                f(yo[b][:, 0:512], bk[5], ACT.Copy)
                f(yo[b][:, 512:D], bk[6], ACT.Copy).then_inc(ey_taken, 1)
                if nxt:
                    maybe(act, more, lambda: weight_high(W_DOWN, n + 1))

            act.wait_ge(h_ready, NT)
            weight_high(W_GATE, 0)
            act.wait_ge(lists_ready, 1)
            x_high(0, 0)
            weight_high(W_UP, 0)
            weight_high(W_DOWN, 0)
            with act.Fori(0, NE // 2 - 1) as i:
                for b in range(2):
                    act_block(act.snap(i * 2 + b), b, i * 2 + (b + 1), True, None)
            act_block(NE - 2, 0, NE - 1, True, None)
            act.wait_ge(more_stored, 16)
            n_more = act.value_load(more_scr[0:1, 2:3], min_val=0, max_val=MAXX)
            act_block(NE - 1, 1, NE, True, n_more > 0)
            further_blocks(act, n_more, lambda i, b: act_block(
                act.snap(i * 2 + (NE + b)), b, i * 2 + (NE + b + 1), True, n_more > i * 2 + (b + 1)))
            for t in range(NT):
                b, r = t % 3, rows(t)
                act.wait_ge(f_sum, t + 1)
                f(f0[b][0:r, :], fh[b][0:r, :], ACT.Square, accum_out=ss4[0:r, b:b + 1])
                act.drain()
                f(rstd4[0:r, b:b + 1], ss4[0:r, b:b + 1], ACT.Sqrt, scale=1.0 / D, bias=eps_t[0:r, :]) \
                    .then_inc(f_rms, 1)

        @block.vector
        def _(dve):
            def tt(out, x, y, op):
                return dve.tensor_tensor(out, x, y, op)

            def bc(x, n):
                return x.unsqueeze(2).broadcast_to([x.shape[0], x.shape[1], n])

            dve.sem_inc(xn_made, 2)
            dve.sem_inc(nT_made, 2)
            dve.wait_ge(par_ready, 1)
            dve.tensor_copy(par[:, :], bk[6][:, 0:48])
            dve.tensor_copy(dwT[:, :], bk[6][:, 64:64 + CW * CC])
            dve.drain()

            def norm_tile(b, r, t):
                dve.wait_ge(x_rms, t + 1)
                dve.reciprocal(rstd[b][0:r, :], rstd[b][0:r, :])
                dve.drain()
                dve.tensor_scalar(xn[b][0:r, :], xt[b][0:r, :], rstd[b][0:r, :], None, ALU.mult) \
                    .then_inc(xn_made, 1)

            def take_tile(b, r, t, t0):
                dve.wait_ge(xT_ready, t + 1)
                for q in range(2):
                    last = tt(nT[:, 4 * q:4 * q + 4, t0],
                              bk[2 * b + q].rearrange("p (k t) -> p k t", t=P)[:, :, 0:r],
                              bc(par[:, 40 + 4 * q:44 + 4 * q], r), ALU.mult)
                last.then_inc(nT_made, 1)

            norm_tile(0, P, 0)
            with dve.Fori(0, NCH // 2 - 1) as i:
                for b in range(2):
                    norm_tile(1 - b, P, i * 2 + (b + 1))
                    take_tile(b, P, i * 2 + b, bass.ds(i * 256 + b * P, P))
            for t in range(NCH - 2, NT):
                if t + 1 < NT:
                    norm_tile((t + 1) % 2, rows(t + 1), t + 1)
                take_tile(t % 2, rows(t), t, slice(t * P, t * P + rows(t)))
            for h in range(H):
                n, az = Z_JOB[h], absz[h % 2]
                dve.drain()
                dve.wait_ge(proj_ready, n + 1)
                dve.wait_ge(absz_made, h + 1)
                bias = par[:, 16 + h:17 + h]
                for j in range(3):
                    dve.tensor_scalar(minz[:, j * BLK:(j + 1) * BLK], bk[3 * (n % 2) + j][:, 0:BLK], bias,
                                      0.0, ALU.add, ALU.min)
                dve.drain()
                dve.wait_ge(ln_made, h + 1)
                tt(minz, minz, az, ALU.subtract).then_inc(taken[n % 2], 1)
                dve.drain()
                spans = [(c * P, P) for c in range(NCH)] + [(SEQ + b * NS, NS) for b in range(NB)]
                for t0, n_t in spans:
                    last = dve.tensor_tensor_scan(az[:, t0:t0 + n_t], ones[:, 0:n_t], minz[:, t0:t0 + n_t], 0.0,
                                                  ALU.mult, ALU.add)
                last.then_inc(b_made, 1)
            for c in range(CC):
                n = 1 + H + CC + c
                dve.wait_ge(proj_ready, n + 1)
                dve.wait_ge(taken[n % 2], n // 2)
                for dst, src in u_parts(c, n):
                    last = tt(dst, src, dst, ALU.mult)
                last.then_inc(taken[n % 2], 1)
                dve.drain().then_inc(u_made, 1)
            dve.wait_ge(sc_T, 1)
            us = u[:, :, UP:UW].rearrange("p c (b w) -> p c b w", w=US)
            for hf in range(2):
                for c in range(CC):
                    last = dve.tensor_copy(us[:, c, 4 * hf:4 * hf + 4, 0:PAD],
                                           bk[6 + hf][:, c * 4 * PAD:(c + 1) * 4 * PAD]
                                           .rearrange("p (b w) -> p b w", w=PAD))
            last.then_inc(sc_taken, 1)
            dve.drain()
            dve.wait_ge(u_padded, 1)
            dve.wait_ge(table_filled, 16)
            ysamp = ybuf[:, :, SEQ:T].rearrange("p c (b s) -> p c b s", s=NS)
            for c in range(CC):
                tap, db = dwT[:, c:c + 1], par[:, 20 + c:21 + c]
                dve.tensor_scalar(ybuf[:, c, 0:SEQ], u[:, c, 0:SEQ], tap, db, ALU.mult, ALU.add)
                dve.tensor_scalar(ysamp[:, c], us[:, c, :, 0:NS], tap, db, ALU.mult, ALU.add)
            with dve.Fori(1, CW) as w:
                dve.drain()
                for c in range(CC):
                    tap = dwT[:, bass.ds(w * CC + c, 1)]
                    dve.scalar_tensor_tensor(ybuf[:, c, 0:SEQ], u[:, c, bass.ds(w, SEQ)], tap, ybuf[:, c, 0:SEQ],
                                             ALU.mult, ALU.add)
                    dve.scalar_tensor_tensor(ysamp[:, c], us[:, c, :, bass.ds(w, NS)], tap, ysamp[:, c],
                                             ALU.mult, ALU.add)
            dve.drain().then_inc(conv_made, 1)
            for j in range(3):
                dve.wait_ge(mean_ready, j + 1)
                v = ybuf[:, :, j * BLK:(j + 1) * BLK]
                mean = bk[6][:, 0:BLK].unsqueeze(1).broadcast_to([P, CC, BLK])
                tt(v, v, mean, ALU.subtract).then_inc(centred, 1)
                dve.wait_ge(std_ready, j + 1)
                dve.reciprocal(stdb[j], stdb[j])
                dve.drain()
                tt(v, v, stdb[j].unsqueeze(1).broadcast_to([P, CC, BLK]), ALU.mult).then_inc(normed, 1)

            dve.wait_ge(attn_zero, 1)
            dve.memset(state[:, :, :], 0.0)
            dve.drain().then_inc(s_made, 1)
            dve.sem_inc(lev_taken, 2)
            dve.sem_inc(oT_taken, 1)

            def halves(x, m, n_t=P):
                v = x.rearrange("p h (n z) -> p (h n) z", z=2 * m) if n_t == P else x
                return v[..., 0:m], v[..., m:2 * m], v[..., m - 1:m]

            def prepare(c, b, loaded):
                dve.wait_ge(chunk_loaded[b], loaded)
                q, k, B = (qkb[b][:, w, :, :] for w in range(3))
                for l in range(LV):
                    m = 64 >> l
                    le, ri = lev_halves(l, m)
                    bl, br_, bm = halves(B, m)
                    mid = bm.broadcast_to([P, H * P // (2 * m), m])
                    tt(ri, br_, mid, ALU.subtract)
                    tt(le, mid, bl, ALU.subtract).then_inc(diff_made, 1)
                tt(kdT[:, :, :], B[:, :, P - 1:P].broadcast_to([P, H, P]), B, ALU.subtract).then_inc(diff_made, 1)
                for l in range(LV):
                    m = 64 >> l
                    le, ri = lev_halves(l, m)
                    dve.wait_ge(exp_made, c * (LV + 2) + (l + 1))
                    tt(ri, ri, halves(q, m)[1], ALU.mult)
                    tt(le, le, halves(k, m)[0], ALU.mult)
                dve.wait_ge(exp_made, c * (LV + 2) + (LV + 2))
                tt(qe[:, :, :], q, ebuf[:, :, :], ALU.mult)
                tt(kdT[:, :, :], kdT[:, :, :], k, ALU.mult).then_inc(prep_made, 1)

            def chunk(c, b, i, t0, nxt):
                for l in range(LV + 2):
                    x = (LV + 2) * b + l
                    src = bk[2 + x % 2]
                    dve.wait_ge(lev_ready, c * (LV + 2) + (l + 1))
                    settle(dve)
                    take_level(l, src, P)
                dve.wait_ge(ds_ready, c + 1)
                for h in range(H):
                    last = dve.scalar_tensor_tensor(state[:, h, :], state[:, h, :], ebuf[:, h, P - 1:P],
                                                    bk[6 + h // 2][:, DV * (h % 2):DV * (h % 2 + 1)],
                                                    ALU.mult, ALU.add)
                last.then_inc(s_made, 1)
                dve.wait_ge(o_rms, c + 1)
                dve.wait_ge(vrc_loaded[b], i * 32 + 32)
                dve.reciprocal(rstd4, rstd4)
                dve.drain()
                for h in range(H):
                    last = dve.scalar_tensor_tensor(onorm[:, h * DV:(h + 1) * DV],
                                                    bk[4 + h // 2][:, DV * (h % 2):DV * (h % 2 + 1)],
                                                    rstd4[:, h:h + 1], vrbuf[:, b, 1, h * DV:(h + 1) * DV],
                                                    ALU.mult, ALU.mult)
                last.then_inc(on_made, 1)
                if nxt is not None:
                    prepare(c + 1, 1 - b, nxt)
                else:
                    prepare_samples()
                take_oT(c + 1, P, t0)

            def take_oT(ready, r, t0):
                dve.wait_ge(oT_ready, ready)
                for q in range(2):
                    last = tt(oT[:, 4 * q:4 * q + 4, t0],
                              bk[4 + q].rearrange("p (k t) -> p k t", t=P)[:, :, 0:r],
                              bc(par[:, 32 + 4 * q:36 + 4 * q], r), ALU.mult)
                last.then_inc(oT_taken, 1)

            def lev_halves(l, m):
                v = lev[:, l, :].rearrange("p (n z) -> p n z", z=2 * m)
                return v[:, :, 0:m], v[:, :, m:2 * m]

            def take_level(l, src, r):
                if l < LV:
                    m, n = 64 >> l, r // (2 * (64 >> l))
                    for h in range(H):
                        dst = attn[0:r, h, 0:r].rearrange("p (n z) -> p n z", z=2 * m)[:, :, m:2 * m]
                        last = dve.copy_predicated(
                            dst, masks[0:r, l * 64:l * 64 + r // 2].rearrange("p (n i) -> p n i", i=m),
                            src[0:r, h * (r // 2):(h + 1) * (r // 2)].rearrange("p (n i) -> p n i", i=m))
                    last.then_inc(lev_taken, 1)
                    dve.drain()
                elif l == LV:
                    for h in range(H):
                        last = dve.copy_predicated(attn[0:r, h, 0:r], masks[0:r, LV * 64:LV * 64 + r],
                                                   src[0:r, h * r:(h + 1) * r])
                    last.then_inc(lev_taken, 1)
                    dve.drain()
                else:
                    dve.tensor_copy(kdn[0:r, :], src[0:r, :]).then_inc(lev_taken, 1)

            R = S_T
            e0, l0 = NCH * (LV + 2), NCH * (LV + 2)

            def prepare_samples():
                dve.wait_ge(chunk_loaded[0], 48 * (NCH // 2 + 1))
                q, k, B = (qkb[0][:, w, :, 0:R] for w in range(3))

                def samp(x, m):
                    v = x.rearrange("p h (n z) -> p h n z", z=2 * m)
                    return v[:, :, :, 0:m], v[:, :, :, m:2 * m], v[:, :, :, m - 1:m]

                def samp_lev(l):
                    return lev[:, l, :].rearrange("p (h t) -> p h t", h=H)[:, :, 0:R]

                for l in (LV - 2, LV - 1):
                    m = 64 >> l
                    for h in range(H):
                        le, ri, _ = samp(samp_lev(l)[:, h:h + 1], m)
                        bl, br_, bm = samp(B[:, h:h + 1], m)
                        mid = bm[:, 0].broadcast_to([P, R // (2 * m), m])
                        tt(ri[:, 0], br_[:, 0], mid, ALU.subtract)
                        last = tt(le[:, 0], mid, bl[:, 0], ALU.subtract)
                    last.then_inc(diff_made, 1)
                for h in range(H):
                    bb = B[:, h, :].rearrange("p (n z) -> p n z", z=NS)
                    last = tt(kdT[:, h, 0:R].rearrange("p (n z) -> p n z", z=NS),
                              bb[:, :, NS - 1:NS].broadcast_to([P, NB, NS]), bb, ALU.subtract)
                last.then_inc(diff_made, 1)
                for x, l in enumerate((LV - 2, LV - 1)):
                    m = 64 >> l
                    dve.wait_ge(exp_made, e0 + x + 1)
                    for h in range(H):
                        le, ri, _ = samp(samp_lev(l)[:, h:h + 1], m)
                        _, qr, _ = samp(q[:, h:h + 1], m)
                        kl, _, _ = samp(k[:, h:h + 1], m)
                        tt(ri[:, 0], ri[:, 0], qr[:, 0], ALU.mult)
                        tt(le[:, 0], le[:, 0], kl[:, 0], ALU.mult)
                dve.wait_ge(exp_made, e0 + 4)
                tt(qe[:, :, 0:R], q, ebuf[:, :, 0:R], ALU.mult)
                tt(kdT[:, :, 0:R], kdT[:, :, 0:R], k, ALU.mult).then_inc(prep_made, 1)

            prepare(0, 0, 48)
            with dve.Fori(0, NCH // 2 - 1) as i:
                for b in range(2):
                    chunk(dve.snap(i * 2 + b), b, i, bass.ds(i * 256 + b * P, P), i * 48 + 48 * (b + 1))
            for b in range(2):
                c = NCH - 2 + b
                chunk(c, b, NCH // 2 - 1, slice(c * P, (c + 1) * P), 48 * NCH // 2 if b == 0 else None)
            dve.memset(attn[0:R, :, 0:R], 0.0)
            dve.memset(flat(gwork)[:, 0:NB * H * R], 0.0)
            dve.drain()
            for b in range(NB):
                last = dve.tensor_copy(lev_qem()[:, b, :, b * NS:(b + 1) * NS], qe[:, :, b * NS:(b + 1) * NS])
            last.then_inc(qem_made, 1)
            for x, l in enumerate((LV - 2, LV - 1, LV, LV + 1)):
                dve.wait_ge(lev_ready, l0 + x + 1)
                take_level(l, bk[2], R)
            dve.drain()
            for b in range(2):
                dve.wait_ge(st_spilled[b], 16 * (H + KC))
            for b in range(NB):
                if b >= 2:
                    dve.wait_ge(sds_ready, b - 1)
                dve.tensor_scalar(lev_kdm()[b % 2][0:R, :], kdn[0:R, :], rowmask[0:R, b:b + 1], None, ALU.mult) \
                    .then_inc(kdm_made, 1)
                if b >= 1:
                    new_state(dve, b - 1)
            new_state(dve, NB - 1)
            dve.wait_ge(o_rms, NCH + 1)
            dve.wait_ge(vrc_loaded[0], 32 * (NCH // 2 + 1))
            dve.reciprocal(rstd4[0:R, :], rstd4[0:R, :])
            dve.drain()
            for h in range(H):
                last = dve.scalar_tensor_tensor(onorm[0:R, h * DV:(h + 1) * DV], bk[4 + h][0:R, 0:DV],
                                                rstd4[0:R, h:h + 1], vrbuf[0:R, 0, 1, h * DV:(h + 1) * DV],
                                                ALU.mult, ALU.mult)
            last.then_inc(on_made, 1)
            take_oT(NCH + 1, R, slice(SEQ, T))

            for j in range(KC):
                dve.wait_ge(gates_sig, j + 1)
                dve.wait_ge(conv_ready, j + 1)
                for q in range(3):
                    t0 = slice(q * BLK, (q + 1) * BLK)
                    last = tt(mixT[:, j, t0], bk[q][:, 0:BLK], st[j % 2][:, t0], ALU.mult)
                last.then_inc(conv_taken, 1)
                dve.wait_ge(gla_ready, j + 1)
                for q in range(3):
                    t0 = slice(q * BLK, (q + 1) * BLK)
                    tt(ggate[j % 2][:, t0], bk[3 + q][:, 0:BLK], ggate[j % 2][:, t0], ALU.mult)
                dve.drain()
                tt(mixT[:, j, :], mixT[:, j, :], ggate[j % 2], ALU.add).then_inc(mix_made, 1)

            dve.wait_ge(small_w, 16 * 5)
            dve.wait_ge(const_ready, 4)
            dve.memset(gl[:, NG:8], -BIG)
            for t in range(NT + 2):
                if 1 <= t <= NT:
                    b, r = (t - 1) % 2, rows(t - 1)
                    dve.wait_ge(hT_ready, t)
                    for q in range(2):
                        last = dve.tensor_copy(hnT[b][:, 4 * q:4 * q + 4, 0:r],
                                               bk[4 + q].rearrange("p (k t) -> p k t", t=P)[:, :, 0:r])
                    last.then_inc(hnT_made, 1)
                if t < NT:
                    b, r = t % 2, rows(t)
                    dve.wait_ge(hx_loaded[b], 16 * (t // 2 + 1))
                    dve.wait_ge(h_ready, t + 1)
                    if t >= 2:
                        dve.wait_ge(h_spilled[b], 32 * (t // 2))
                    for hf in range(2):
                        last = tt(hh[b][0:r, 512 * hf:512 * hf + 512], bk[2 * b + hf][0:r, :],
                                  hx[b][0:r, 512 * hf:512 * hf + 512], ALU.add)
                    last.then_inc(h_made, 1)
                    dve.wait_ge(h_squared, t + 1)
                    dve.reciprocal(rstd[b][0:r, :], rstd[b][0:r, :])
                    dve.drain()
                    dve.scalar_tensor_tensor(hn[b][0:r, :], hh[b][0:r, :], rstd[b][0:r, :], nffn[0:r, :],
                                             ALU.mult, ALU.mult).then_inc(hn_made, 1)
                if 1 <= t <= NT:
                    b, r = (t - 1) % 2, rows(t - 1)
                    dve.wait_ge(logit_ready, t)
                    pick(dve, t - 1, r, mpick[b])
                if t >= 2:
                    b, r = t % 2, rows(t - 2)
                    dve.wait_ge(rank_ready, t - 1)
                    dve.tensor_tensor(rk[0:r, :], bk[7][0:r, 0:NE], slot0[0:r, :], ALU.add)
                    dve.drain()
                    for k in range(2):
                        dve.tensor_tensor_reduce((junk, junk2)[k][0:r, :],
                                                 rk[0:r, :], mpick[b][0:r, k, :], 1.0, 0.0, ALU.mult, ALU.add,
                                                 slotf[0:r, k:k + 1])
                    dve.tensor_tensor(macc[0:r, :], macc[0:r, :], mpick[b][0:r, 2, :], ALU.add)
                    dve.drain()
                    dve.tensor_copy(sloti[0:r, t - 2, :], slotf[0:r, :]).then_inc(slot_made, 1)
                    dve.drain()
            dve.wait_ge(count_ready, 1)
            dve.tensor_copy(cnt, bk[7][:, 0:NE])
            dve.wait_ge(lists_loaded, 16)
            dve.tensor_copy(lst_f, lst_i).then_inc(lists_f, 1)
            dve.wait_ge(lists_T, 1)
            dve.tensor_copy(lst_tok, bk[6][:, 0:NE])
            dve.tensor_copy(lst_pair, bk[6][:, P:P + NE])
            dve.drain().then_inc(lists_ready, 1)
            def weight_low(kind, n, halves=range(2)):
                for hf in halves:
                    cs = slice(hf * HALF, (hf + 1) * HALF)
                    dve.wait_ge(wH_made[kind], n * 2 + (hf + 1))
                    tt(wL[kind][:, cs], RAWV[kind][:, cs], wH[kind][:, cs].bitcast(F32), ALU.subtract) \
                        .then_inc(wL_made[kind], 1)

            def x_low(n, b):
                dve.wait_ge(xeH_made, n + 1)
                for q in range(2):
                    last = tt(xeL[:, b, 4 * q:4 * q + 4, :].rearrange("p k t -> p (k t)"), bk[q],
                              xeH[:, b, 4 * q:4 * q + 4, :].rearrange("p k t -> p (k t)").bitcast(F32), ALU.subtract)
                last.then_inc(xe_made, 1)

            def dve_block(n, b, nxt, more):
                if nxt:
                    maybe(dve, more, lambda: weight_low(W_GATE, n + 1, [0]))
                dve.wait_ge(sg_made, n + 1)
                dve.wait_ge(eu_done, n + 1)
                tt(hid, bk[3], sgate, ALU.mult).then_inc(hid_made, 1)
                if nxt:
                    maybe(dve, more, lambda: weight_low(W_GATE, n + 1, [1]))
                dve.wait_ge(hidTH_made, n + 1)
                tt(hidTL[:, :, :].rearrange("p k t -> p (k t)"), bk[4],
                   hidTH[:, :, :].rearrange("p k t -> p (k t)").bitcast(F32), ALU.subtract).then_inc(hidT_made, 1)
                if nxt:
                    def work():
                        x_low(n + 1, 1 - b)
                        weight_low(W_UP, n + 1)
                        weight_low(W_DOWN, n + 1)
                    maybe(dve, more, work)

            weight_low(W_GATE, 0)
            x_low(0, 0)
            weight_low(W_UP, 0)
            weight_low(W_DOWN, 0)
            dve.wait_ge(const_ready, 5)
            c3 = cnt[0:16, :].unsqueeze(2).broadcast_to([16, NE, NBX])

            def eb(x):
                return x.rearrange("p (e b) -> p e b", b=NBX)

            tt(eb(m_flag), c3, eb(m_th), ALU.is_gt)
            dve.drain()
            dve.tensor_tensor_scan(m_rank, m_one, m_flag, 0.0, ALU.mult, ALU.add)
            dve.drain()
            dve.tensor_scalar(m_eq, m_rank, jidx[0:16, :], None, ALU.is_equal)
            dve.drain()
            tt(m_eq, m_eq, m_flag, ALU.mult)
            dve.drain()
            dve.tensor_tensor_reduce(m_val, m_eq, m_base, 1.0, 0.0, ALU.mult, ALU.add, m_out[:, 0:1])
            dve.drain()
            dve.tensor_tensor_reduce(m_val, m_eq, m_e, 1.0, 0.0, ALU.mult, ALU.add, m_out[:, 1:2])
            dve.tensor_copy(m_out[:, 2:3], m_rank[:, NF - 1:NF])
            dve.memset(m_out[:, 3:4], 0.0)
            dve.drain()
            dve.tensor_copy(m_int, m_out).then_inc(more_made, 1)
            with dve.Fori(0, NE // 2 - 1) as i:
                for b in range(2):
                    dve_block(dve.snap(i * 2 + b), b, True, None)
            dve_block(NE - 2, 0, True, None)
            dve.wait_ge(more_stored, 16)
            n_more = dve.value_load(more_scr[0:1, 2:3], min_val=0, max_val=MAXX)
            dve_block(NE - 1, 1, True, n_more > 0)
            further_blocks(dve, n_more, lambda i, b: dve_block(
                dve.snap(i * 2 + (NE + b)), b, True, n_more > i * 2 + (b + 1)))

            def f_add(t):
                b, r = t % 3, rows(t)
                dve.wait_ge(f_loaded[b], 48 * (t // 3 + 1))
                dve.scalar_tensor_tensor(fh[b][0:r, :], f0[b][0:r, :], wts[0:r, t, 0:1], fh[b][0:r, :],
                                         ALU.mult, ALU.add)
                dve.drain()
                dve.scalar_tensor_tensor(fh[b][0:r, :], f1[b][0:r, :], wts[0:r, t, 1:2], fh[b][0:r, :],
                                         ALU.mult, ALU.add).then_inc(f_sum, 1)

            f_add(0)
            dve.wait_ge(lists_loaded, 16 * 2)
            for t in range(NT):
                b, r = t % 3, rows(t)
                if t + 1 < NT:
                    f_add(t + 1)
                dve.wait_ge(f_rms, t + 1)
                if t >= 3:
                    dve.wait_ge(f_out[b], 16 * (t // 3))
                dve.reciprocal(rstd4[0:r, b:b + 1], rstd4[0:r, b:b + 1])
                dve.drain()
                dve.scalar_tensor_tensor(fo[b][0:r, :], fh[b][0:r, :], rstd4[0:r, b:b + 1], nfin[0:r, :],
                                         ALU.mult, ALU.mult).then_inc(f_made, 1)


_INS = ["x_prompt", "x_sample", "state_conv", "state_gla", "norm_mix", "w_in", "b_gates", "w_gla_gate_up",
        "b_gla_gate_up", "conv_dw", "conv_db", "conv_ln_g", "conv_ln_b", "w_conv_out", "gla_norm_g", "w_gla_out",
        "w_out", "norm_ffn", "w_router_group", "b_router_group", "w_router_expert", "b_router_expert",
        "w_expert_gate", "w_expert_up", "w_expert_down", "norm_final"]
_OUTS = {"y_prompt": (1, 1024, 1024), "y_sample": (8, 4, 1024), "new_conv_prompt": (1, 1, 30, 512),
         "new_gla_prompt": (1, 1, 4, 128, 256), "new_conv_sample": (1, 8, 30, 512),
         "new_gla_sample": (1, 8, 4, 128, 256)}


def kernel(**inputs):
    import numpy as np
    import concourse.bacc as bacc
    from concourse.bass_utils import run_bass_kernel_spmd as run

    nc = bacc.Bacc("TRN2", target_bir_lowering=False, num_devices=1)
    arrays, a, o = {}, {}, {}
    for name in _INS:
        x = np.ascontiguousarray(inputs[name])
        arrays[f"in_{name}"] = x
        a[name] = nc.dram_tensor(f"in_{name}", x.shape, mybir.dt.from_np(x.dtype), kind="ExternalInput").ap()
    for name, shape in _OUTS.items():
        o[name] = nc.dram_tensor(f"out_{name}", shape, F32, kind="ExternalOutput").ap()
    hybrid_layer(nc, a, o)
    r = run(nc, [arrays], core_ids=[0])
    return tuple(r.results[0][f"out_{name}"] for name in _OUTS)
```
